# Optimizing a Trainium2 kernel written in Bass

```python
import math
import jax, jax.numpy as jnp
from jax import lax
import numpy as np

D_MODEL = 2048
BATCH = 1
SEQ = 256
DEPTH = 2

D_MIX = D_MODEL
D_POOL = D_MIX // 2
POOL_WINDOWS = (2, 4, 8, 16)
N_POOL_GROUPS = len(POOL_WINDOWS)
POOL_C = D_POOL // N_POOL_GROUPS
N_HEADS = 8
NOPE_DIM = 128
ROPE_DIM = 64
V_DIM = 128
D_ATT = N_HEADS * V_DIM
Q_LORA = D_MODEL // 4
KV_LORA = D_MODEL // 4
ROPE_THETA = 10000.0
Q_BLOCK = 128
D_IN = D_POOL + Q_LORA + KV_LORA + ROPE_DIM
D_FF = 5632
CONV_W = 3
PLE_DIM = 256
EPS = 1e-6

kernel_name = 'hybrid_pool_mla_convffn_ple'

def rms_norm(x, g):
    xf = x.astype(jnp.float32)
    y = xf * lax.rsqrt(jnp.mean(xf * xf, axis=-1, keepdims=True) + EPS)
    return (y * g.astype(jnp.float32)).astype(x.dtype)

def rope_tables(positions):
    inv_freq = 1.0 / (ROPE_THETA ** (jnp.arange(0, ROPE_DIM, 2, dtype=jnp.float32) / ROPE_DIM))
    ang = positions.astype(jnp.float32)[..., None] * inv_freq
    return jnp.cos(ang), jnp.sin(ang)

def apply_rope(x, cos, sin):
    half = x.shape[-1] // 2
    xf = x.astype(jnp.float32)
    x1, x2 = xf[..., :half], xf[..., half:]
    return jnp.concatenate([x1 * cos - x2 * sin, x2 * cos + x1 * sin], axis=-1).astype(x.dtype)

def multiscale_pool(u, pool_w, pool_scale):
    B, S, _ = u.shape
    uf = u.astype(jnp.float32)
    cs = jnp.cumsum(uf, axis=1)
    t = jnp.arange(S)
    outs = []
    for g, w in enumerate(POOL_WINDOWS):
        c = cs[..., g * POOL_C:(g + 1) * POOL_C]
        lag = jnp.pad(c, ((0, 0), (w, 0), (0, 0)))[:, :S]
        cnt = jnp.minimum(t + 1, w).astype(jnp.float32)[None, :, None]
        outs.append((c - lag) / cnt)
    pooled = jnp.stack(outs, axis=2)
    diff = (pooled - uf.reshape(B, S, N_POOL_GROUPS, POOL_C)).astype(u.dtype)
    y = jnp.einsum('bsgc,gcd->bsgd', diff, pool_w).reshape(B, S, D_POOL)
    return y * pool_scale

def latent_attention(c_q, c_kv, k_rope_raw, cos, sin, q_norm_g, w_uq, kv_norm_g, w_ukv):
    B, S, _ = c_q.shape
    q = (rms_norm(c_q, q_norm_g) @ w_uq).reshape(B, S, N_HEADS, NOPE_DIM + ROPE_DIM)
    q_nope = q[..., :NOPE_DIM]
    q_rope = apply_rope(q[..., NOPE_DIM:], cos[:, :, None], sin[:, :, None])
    kv = (rms_norm(c_kv, kv_norm_g) @ w_ukv).reshape(B, S, N_HEADS, NOPE_DIM + V_DIM)
    k_nope, v = kv[..., :NOPE_DIM], kv[..., NOPE_DIM:]
    k_rope = apply_rope(k_rope_raw, cos, sin)
    scale = 1.0 / math.sqrt(NOPE_DIM + ROPE_DIM)
    nb = S // Q_BLOCK
    qn = q_nope.reshape(B, nb, Q_BLOCK, N_HEADS, NOPE_DIM).transpose(1, 0, 2, 3, 4)
    qr = q_rope.reshape(B, nb, Q_BLOCK, N_HEADS, ROPE_DIM).transpose(1, 0, 2, 3, 4)
    k_pos = jnp.arange(S)

    def block(args):
        qn_b, qr_b, bi = args
        s = (jnp.einsum('bqhd,bkhd->bhqk', qn_b, k_nope).astype(jnp.float32)
             + jnp.einsum('bqhr,bkr->bhqk', qr_b, k_rope).astype(jnp.float32)) * scale
        q_pos = bi * Q_BLOCK + jnp.arange(Q_BLOCK)
        s = jnp.where(q_pos[:, None] >= k_pos[None, :], s, -jnp.inf)
        pr = jax.nn.softmax(s, axis=-1).astype(v.dtype)
        return jnp.einsum('bhqk,bkhd->bqhd', pr, v)

    out = lax.map(block, (qn, qr, jnp.arange(nb)))
    return out.transpose(1, 0, 2, 3, 4).reshape(B, S, D_ATT)

def causal_depthwise_conv(x, w, b):
    C = x.shape[-1]
    y = lax.conv_general_dilated(x, w[:, None, :].astype(x.dtype), window_strides=(1,),
                                 padding=[(CONV_W - 1, 0)],
                                 dimension_numbers=('NWC', 'WIO', 'NWC'),
                                 feature_group_count=C)
    return y + b

def conv_gated_ffn(x, w_up, conv_w, conv_b, w_down):
    gu = x @ w_up
    gate, up = gu[..., :D_FF], gu[..., D_FF:]
    gate = causal_depthwise_conv(gate, conv_w, conv_b)
    return (jax.nn.silu(gate) * up) @ w_down

def setup_inputs(seed: int = 0) -> dict:
    key = jax.random.key(seed)
    ks = jax.random.split(key, 24)
    f32 = jnp.float32

    def nrm(k, shape, fan_in):
        return jax.random.normal(k, shape, f32) * (fan_in ** -0.5)

    def gain(k, shape):
        return 1.0 + 0.02 * jax.random.normal(k, shape, f32)

    return {
        'x': jax.random.normal(ks[0], (BATCH, SEQ, D_MODEL), f32),
        'p': jax.random.normal(ks[1], (DEPTH, BATCH, SEQ, PLE_DIM), f32),
        'positions': jnp.broadcast_to(jnp.arange(SEQ, dtype=jnp.int32), (BATCH, SEQ)),
        'norm_mix_g': gain(ks[2], (DEPTH, D_MODEL)),
        'w_in': nrm(ks[3], (DEPTH, D_MODEL, D_IN), D_MODEL),
        'pool_w': nrm(ks[4], (DEPTH, N_POOL_GROUPS, POOL_C, POOL_C), POOL_C),
        'pool_scale': gain(ks[5], (DEPTH, D_POOL)),
        'q_norm_g': gain(ks[6], (DEPTH, Q_LORA)),
        'w_uq': nrm(ks[7], (DEPTH, Q_LORA, N_HEADS * (NOPE_DIM + ROPE_DIM)), Q_LORA),
        'kv_norm_g': gain(ks[8], (DEPTH, KV_LORA)),
        'w_ukv': nrm(ks[9], (DEPTH, KV_LORA, N_HEADS * (NOPE_DIM + V_DIM)), KV_LORA),
        'w_out': nrm(ks[10], (DEPTH, D_MIX, D_MODEL), D_MIX),
        'norm_ffn_g': gain(ks[11], (DEPTH, D_MODEL)),
        'w_up': nrm(ks[12], (DEPTH, D_MODEL, 2 * D_FF), D_MODEL),
        'conv_w': nrm(ks[13], (DEPTH, CONV_W, D_FF), CONV_W),
        'conv_b': 0.01 * jax.random.normal(ks[14], (DEPTH, D_FF), f32),
        'w_down': nrm(ks[15], (DEPTH, D_FF, D_MODEL), D_FF),
        'norm_ple_g': gain(ks[16], (DEPTH, D_MODEL)),
        'w_ple': nrm(ks[17], (DEPTH, PLE_DIM, D_MODEL), PLE_DIM),
        'w_ple_gate': nrm(ks[18], (DEPTH, D_MODEL, D_MODEL), D_MODEL),
        'final_norm_g': gain(ks[19], (D_MODEL,)),
    }

def reference(x, p, positions, norm_mix_g, w_in, pool_w, pool_scale, q_norm_g, w_uq,
              kv_norm_g, w_ukv, w_out, norm_ffn_g, w_up, conv_w, conv_b, w_down,
              norm_ple_g, w_ple, w_ple_gate, final_norm_g):
    cos, sin = rope_tables(positions)
    o1 = D_POOL
    o2 = o1 + Q_LORA
    o3 = o2 + KV_LORA
    h = x
    for i in range(DEPTH):
        u = rms_norm(h, norm_mix_g[i]) @ w_in[i]
        y_pool = multiscale_pool(u[..., :o1], pool_w[i], pool_scale[i])
        y_att = latent_attention(u[..., o1:o2], u[..., o2:o3], u[..., o3:], cos, sin,
                                 q_norm_g[i], w_uq[i], kv_norm_g[i], w_ukv[i])
        h = h + jnp.concatenate([y_pool, y_att], axis=-1) @ w_out[i]
        h = h + conv_gated_ffn(rms_norm(h, norm_ffn_g[i]), w_up[i], conv_w[i], conv_b[i], w_down[i])
        gate = jax.nn.sigmoid(rms_norm(h, norm_ple_g[i]) @ w_ple_gate[i])
        h = h + (p[i] @ w_ple[i]) * gate
    return rms_norm(h, final_norm_g)


_drawn_inputs = setup_inputs


def setup_inputs(seed=0):
    import zlib

    import numpy as np

    out = dict(_drawn_inputs(seed))
    spreads = {}
    factors = {'norm_mix_g': 3.844,
     'pool_scale': 3.944,
     'q_norm_g': 8.0,
     'kv_norm_g': 8.0,
     'norm_ffn_g': 3.499,
     'conv_b': 8.0,
     'norm_ple_g': 8.0,
     'final_norm_g': 2.917}
    for name, (base, spread) in spreads.items():
        noise = np.random.default_rng([zlib.crc32(name.encode()), seed]).standard_normal(out[name].shape)
        drawn = base * np.exp(spread * noise) if base else spread * noise
        out[name] = __import__('jax').numpy.asarray(drawn.astype(out[name].dtype))
    for name, factor in factors.items():
        out[name] = (out[name] * factor).astype(out[name].dtype)
    return out
```

```python
from contextlib import ExitStack

import numpy as np

import concourse.bass as bass
from concourse import mybir

P = 128
F32 = mybir.dt.float32
F32R = mybir.dt.float32r
I32 = mybir.dt.int32
ACT = mybir.ActivationFunctionType
ALU = mybir.AluOpType

POOL_WINDOWS = (2, 4, 8, 16)
HEADS, NOPE, ROPE, VDIM = 8, 128, 64, 128
THETA = 10000.0
EPS = 1e-6
MASKED = -3.0e38

CHUNK = 2048
HALF = CHUNK // 2
RAW_SLOTS = 3
HALF_SLOTS = 6
AHEAD = 4
POOL_SETUP = 42 + 4 * len(POOL_WINDOWS) + 4 * len(POOL_WINDOWS)
DVE_REDUCED = 18
BLK = 512
T_BANKS = 4


def layer_plan(d_model, d_ff):
    n_blk = d_model // BLK
    units = d_ff // BLK
    kt = d_model // P
    per_block = kt // 4
    c, chunk = 0, {}
    for name, n in (("cq", per_block), ("ckv", per_block), ("kr", 1), ("pool", 2 * per_block), ("uq", 3),
                    ("ukv", 4), ("poolw", 2), ("out", n_blk * per_block), ("ffn", units * 3 * per_block),
                    ("ple", n_blk * per_block + 2)):
        chunk[name] = c
        c += n
    b, block = 0, {}
    for name, n in (("cq", 1), ("ckv", 1), ("kr", 1), ("pool", 2), ("qrope", 1), ("qnope", 2), ("knope", 2),
                    ("v", 2), ("poolw", 2), ("out", n_blk), ("ffn", units * (2 + n_blk)), ("ple", 2 * n_blk)):
        block[name] = b
        b += n
    j, job = 0, {}
    for name, n in (("mix", kt // 2), ("cq", 2), ("kr", 1), ("ckv", 2), ("diff", 4), ("qrope", 2),
                    ("heads", 3 * HEADS), ("ffn_norm", kt // 2), ("ffn", 4 * units), ("p", 1), ("ple_norm", kt // 2)):
        job[name] = j
        j += n
    last = {}
    for name, n in (("cq", 1), ("ckv", 1), ("pool", 2)):
        for i in range(n):
            last[block[name] + i] = 2 * (chunk[name] + (i + 1) * per_block) - 1
    last[block["kr"]] = 2 * chunk["kr"]
    last[block["qrope"]] = 2 * chunk["uq"] + 1
    last[block["qnope"] + 1] = 2 * chunk["uq"] + 5
    last[block["knope"] + 1] = 2 * chunk["ukv"] + 3
    last[block["v"] + 1] = 2 * chunk["ukv"] + 7
    for i in range(2):
        last[block["poolw"] + i] = 2 * (chunk["poolw"] + i)
    for name, ends in (("out", (11, 15, 23, 31)), ("ffn", (7, 15, 23, 31, 33, 35, 37, 39)),
                       ("ple", (1, 1, 9, 17, 19, 19, 27, 35))):
        for i, m in enumerate(ends):
            last[block[name] + i] = 2 * chunk[name] + m
    for i in range(n_blk):
        last[block["ple"] - n_blk + i] = 2 * (chunk["ple"] - n_blk + i) + 1
    return dict(last=last, n_blk=n_blk, units=units, kt=kt, chunk=chunk, chunks=c, block=block, blocks=b, job=job, jobs=j)


def head_jobs(first):
    s, t, y, n = {}, {}, {}, first
    for i in range(HEADS + 2):
        if i < HEADS:
            s[i] = n
            n += 1
        if i >= 2:
            y[i - 2] = n
            n += 1
        if 1 <= i <= HEADS:
            t[i - 1] = n
            n += 1
    return s, t, y


def build(nc, x, p, positions, norm_mix_g, w_in, pool_w, pool_scale, q_norm_g, w_uq, kv_norm_g, w_ukv,
          w_out, norm_ffn_g, w_up, conv_w, conv_b, w_down, norm_ple_g, w_ple, w_ple_gate, final_norm_g, out):
    L, D, _ = w_in.shape
    S = x.shape[1]
    D_FF = w_down.shape[1]
    D_POOL = pool_scale.shape[1]
    LORA = w_uq.shape[1]
    PLE = w_ple.shape[1]
    TT = S // P
    plan = layer_plan(D, D_FF)
    N_BLK, UNITS, KT = plan["n_blk"], plan["units"], plan["kt"]
    CH, BL, JB = plan["chunk"], plan["block"], plan["job"]
    CHUNKS, BLOCKS, JOBS = plan["chunks"], plan["blocks"], plan["jobs"]
    LKT = LORA // P
    PKT = D_POOL // P
    SCALE = float(NOPE + ROPE) ** -0.5
    assert TT == 2 and LORA == BLK and D_POOL == 2 * BLK and PLE == 2 * P and LKT == 4
    assert CHUNKS % RAW_SLOTS == 0 and 2 * CHUNKS % HALF_SLOTS == 0 and 12 % RAW_SLOTS == 0
    assert BLOCKS % 2 == 0 and JOBS % T_BANKS == 0
    JS, JT, JY = head_jobs(JB["heads"])
    LAST = plan["last"]

    G_MIX, G_FFN, G_PLE = 0, KT, 2 * KT
    POOL_S = 3 * KT
    FKT = D_FF // P
    TAP = [POOL_S + PKT + t * FKT for t in range(3)]
    BIAS = TAP[2] + FKT
    G_Q = BIAS + FKT
    G_KV = G_Q + LKT
    N_PRM = G_KV + LKT
    ROWS_G = 3 * KT + PKT

    with ExitStack() as ctx:
        def sb(name, shape, dt=F32, scope=ctx):
            return scope.enter_context(nc.sbuf_tensor(name, shape, dt))

        def sem(name):
            return ctx.enter_context(nc.semaphore(name))

        raw = sb("raw", [P, RAW_SLOTS, CHUNK])
        w_hi = sb("w_hi", [P, HALF_SLOTS, HALF], F32R)
        w_lo = sb("w_lo", [P, HALF_SLOTS, HALF], F32R)
        xa = (sb("xa_hi", [P, KT, S], F32R), sb("xa_lo", [P, KT, S], F32R))
        xb = (sb("xb_hi", [P, KT, S], F32R), sb("xb_lo", [P, KT, S], F32R))
        h = sb("h", [P, TT, D])
        ident = sb("ident", [P, P])
        mask = sb("mask", [P, 2 * P])
        band_hi = sb("band_hi", [P, len(POOL_WINDOWS), 3 * P], F32R)
        band_lo = sb("band_lo", [P, len(POOL_WINDOWS), 16], F32R)
        cos = sb("cos", [P, TT, ROPE // 2])
        sin = sb("sin", [P, TT, ROPE // 2])
        prm_all = sb("prm_all", [P, L, N_PRM])
        prm = sb("prm", [P, N_PRM])
        krt = (sb("krt_hi", [P, 2, S], F32R), sb("krt_lo", [P, 2, S], F32R))
        sumsq = sb("sumsq", [P, TT, N_BLK])
        sumsq_lat = sb("sumsq_lat", [P, 2, TT])
        rstd = {n: sb(f"rstd_{n}", [P, TT]) for n in ("mix", "q", "kv", "ffn", "ple", "final")}
        part = sb("part", [P, TT, 2])
        mean = sb("mean", [P, TT])
        consts = sb("consts", [P, 5, TT])
        C_D, C_LORA, C_EPS, C_POWER, C_HALF = range(5)
        mx = sb("mx", [P, 2, TT])
        nmx = sb("nmx", [P, 2, TT])
        psums = sb("psums", [P, 2, TT])
        prec = sb("prec", [P, 2, TT])

        with ExitStack() as scope:
            rows_g = sb("rows_g", [ROWS_G, L, P], scope=scope)
            rows_c = [sb(f"rows_c{i}", [2 * FKT, L, P], scope=scope) for i in range(2)]
            band = sb("band", [P, len(POOL_WINDOWS), 3 * P], scope=scope)
            inv_cnt = sb("inv_cnt", [P, 16], scope=scope)
            pos_i = sb("pos_i", [P, TT], I32, scope=scope)
            pos_f = sb("pos_f", [P, TT], scope=scope)
            inv_freq = sb("inv_freq", [P, ROPE // 2], scope=scope)
            ang = sb("ang", [P, TT, ROPE // 2], scope=scope)
            turns = sb("turns", [P, 2, TT, ROPE // 2], scope=scope)
            red = sb("red", [P, 2, TT, ROPE // 2], scope=scope)
            sq_setup = sb("sq_setup", [P, TT, BLK], scope=scope)
        with ExitStack() as scope:
            with ExitStack() as early:
                lat = sb("lat", [P, 2, TT, BLK], scope=early)
                kr_tok = sb("kr_tok", [P, TT, P], scope=early)
                kr_in = sb("kr_in", [P, TT, ROPE], scope=early)
                kr_tmp = sb("kr_tmp", [P, 2, TT, ROPE // 2], scope=early)
                sq_lat = sb("sq_lat", [P, TT, BLK], scope=early)
            v = (sb("v_hi", [P, TT, HEADS * VDIM], F32R, scope=scope),
                 sb("v_lo", [P, TT, HEADS * VDIM], F32R, scope=scope))
            qrt = (sb("qrt_hi", [P, HEADS // 2, S], F32R, scope=scope),
                   sb("qrt_lo", [P, HEADS // 2, S], F32R, scope=scope))
            up_ = (sb("upool_hi", [P, TT, BLK], F32R, scope=scope),
                   sb("upool_lo", [P, TT, BLK], F32R, scope=scope))
            with ExitStack() as early:
                qr_tok = sb("qr_tok", [P, TT, BLK], scope=early)
                qr_tmp = sb("qr_tmp", [P, 2, BLK // 2], scope=early)
            prob = sb("prob", [P, 2, 3 * P], scope=scope)
            pt = (sb("pt_hi", [P, 3 * P], F32R, scope=scope), sb("pt_lo", [P, 3 * P], F32R, scope=scope))
        with ExitStack() as scope:
            gate_tok = sb("gate_tok", [P, TT, BLK], scope=scope)
            up_tok = sb("up_tok", [P, TT, BLK], scope=scope)
            conv = sb("conv", [P, 4, S], scope=scope)
            sig = sb("sig", [P, 4, S], scope=scope)
            gt = (sb("gt_hi", [P, 4, S], F32R, scope=scope), sb("gt_lo", [P, 4, S], F32R, scope=scope))
            p_tok = sb("p_tok", [P, TT, PLE], scope=scope)
            ppt = (sb("ppt_hi", [P, 2, S], F32R, scope=scope), sb("ppt_lo", [P, 2, S], F32R, scope=scope))
            sq_h = sb("sq_h", [P, TT, BLK], scope=scope)
        with ExitStack() as scope:
            pw = sb("pw", [P, 2, TT, 2 * BLK], scope=scope)
            sg = sb("sg", [P, 2, TT, BLK], scope=scope)
        with ExitStack() as scope:
            fin_g = sb("fin_g", [P, D], scope=scope)

        acc = [ctx.enter_context(nc.psum_tensor(f"acc{i}", [P, 2, BLK], F32)) for i in range(2)]
        tps = ctx.enter_context(nc.psum_tensor("tps", [P, T_BANKS, BLK], F32))

        raw_landed = [sem(f"raw_landed{i}") for i in range(RAW_SLOTS)]
        slot_seen = sem("slot_seen")
        scores_seen = sem("scores_seen")
        hi_done = sem("hi_done")
        lo_done = sem("lo_done")
        w_used = sem("w_used")
        pair_ready = sem("pair_ready")
        acc_free = [sem(f"acc_free{i}") for i in range(2)]
        t_ready = sem("t_ready")
        t_done = sem("t_done")
        x_landed = [sem(f"x_landed{i}") for i in range(N_BLK)]
        rows_landed = sem("rows_landed")
        conv_landed = sem("conv_landed")
        lat_landed = sem("lat_landed")
        pos_landed = sem("pos_landed")
        p_landed = sem("p_landed")
        fin_landed = sem("fin_landed")
        stored = sem("stored")
        pool_setup = sem("pool_setup")
        dve_setup = sem("dve_setup")
        act_setup = sem("act_setup")
        prm_t = sem("prm_t")
        prm_ready = sem("prm_ready")
        h_ready = sem("h_ready")
        sq_done = sem("sq_done")
        sq_lat_done = sem("sq_lat_done")
        rstd_step = sem("rstd_step")
        rstd_done = sem("rstd_done")
        lat_norm = sem("lat_norm")
        hT_hi = sem("hT_hi")
        lat_hi = sem("lat_hi")
        kr_in_done = sem("kr_in_done")
        kr_step = sem("kr_step")
        kr_hi = sem("kr_hi")
        upool_hi = sem("upool_hi")
        diff_hi = sem("diff_hi")
        qr_step = sem("qr_step")
        qr_hi = sem("qr_hi")
        qk_hi = sem("qk_hi")
        v_hi = sem("v_hi")
        ypool_hi = sem("ypool_hi")
        s_ready = sem("s_ready")
        s_max = sem("s_max")
        e_done = sem("e_done")
        p_rec = sem("p_rec")
        p_norm = sem("p_norm")
        pt_hi = sem("pt_hi")
        y_hi = sem("y_hi")
        conv_step = sem("conv_step")
        silu_done = sem("silu_done")
        conv_done = sem("conv_done")
        tanh_done = sem("tanh_done")
        g_done = sem("g_done")
        g_hi = sem("g_hi")
        g_lo = sem("g_lo")
        p_hi = sem("p_hi")
        ple_step = sem("ple_step")
        fin_done = sem("fin_done")

        LAT_Q, LAT_KV = 0, LKT
        DIFF = 2 * LKT
        Q_T, K_T = 0, HEADS
        HJ = KT // 2

        def half_of(m):
            return m % HALF_SLOTS

        def block_ready(eng, l, b, v=None):
            base = l * (2 * CHUNKS) if v is None else l * (2 * CHUNKS) + v * 24
            eng.wait_ge(w_used, base + (HALF_SLOTS + LAST[b] + 1))

        def scalar_of(col):
            return prm[:, col:col + 1]

        block = ctx.enter_context(nc.Block())

        @block.sync
        def _(sp):
            def load(l, c, pieces):
                slot = c % RAW_SLOTS
                sp.wait_ge(lo_done, 2 * CHUNKS * l + 2 * c + 2)
                sp.sem_inc(slot_seen, 1)
                src, width, shape = pieces
                dst = raw[:, slot, 0:width]
                if shape is not None:
                    dst = dst.rearrange("p (a b) -> p a b", b=shape)
                sp.dma_start(dst, src).then_inc(raw_landed[slot], 16)

            def rows(w, l, k0, nk, cols, n):
                view = w.rearrange("l (k p) n -> l p k n", p=P)
                return view[bass.ds(l, 1), :, bass.ds(k0, nk), bass.ds(cols, n)].rearrange("l p k n -> p (l k) n")

            def square(w, l, k4, col):
                return rows(w, l, 4 * k4, 4, col, BLK), CHUNK, BLK

            def heads_cols(w, l, width, k0, nk, c0, n):
                view = w.rearrange("l (p k) (h c) -> l p (k h) c", k=LKT, c=width)
                return view[bass.ds(l, 1), :, HEADS * k0:HEADS * (k0 + nk), c0:c0 + n].rearrange(
                    "l p k n -> p (l k) n")

            for i, g in enumerate((norm_mix_g, norm_ffn_g, norm_ple_g)):
                sp.dma_start(rows_g[KT * i:KT * (i + 1)], g.rearrange("l (k p) -> k l p", p=P)).then_inc(
                    rows_landed, 16)
            sp.dma_start(rows_g[POOL_S:POOL_S + PKT], pool_scale.rearrange("l (k p) -> k l p", p=P)).then_inc(
                rows_landed, 16)

            with sp.Fori(0, L) as l:
                c = CH["cq"]
                for col in (D_POOL, D_POOL + LORA):
                    for k in range(KT // 4):
                        load(l, c, square(w_in, l, k, col))
                        c += 1
                load(l, c, (rows(w_in, l, 0, KT, D_POOL + 2 * LORA, ROPE), KT * ROPE, ROPE))
                c += 1
                for col in (0, BLK):
                    for k in range(KT // 4):
                        load(l, c, square(w_in, l, k, col))
                        c += 1
                load(l, c, (heads_cols(w_uq, l, NOPE + ROPE, 0, LKT, NOPE, ROPE), CHUNK, ROPE))
                for i in range(2):
                    load(l, c + 1 + i, (heads_cols(w_uq, l, NOPE + ROPE, 2 * i, 2, 0, NOPE), CHUNK, NOPE))
                c += 3
                for c0 in (0, NOPE):
                    for i in range(2):
                        load(l, c, (heads_cols(w_ukv, l, NOPE + VDIM, 2 * i, 2, c0, NOPE), CHUNK, NOPE))
                        c += 1
                for i in range(2):
                    src = pool_w[bass.ds(l, 1), 2 * i:2 * i + 2].rearrange("l g (k p) n -> p (l g k) n", p=P)
                    load(l, c, (src, HALF, 2 * P))
                    c += 1
                for j, k in ([(j, k) for k0 in (0, 2) for j in (0, 1) for k in (k0, k0 + 1)]
                             + [(j, k) for j in (2, 3) for k in range(4)]):
                    load(l, c, square(w_out, l, k, j * BLK))
                    c += 1

                def gate_up(l, u, c):
                    for col in (0, D_FF):
                        for k in range(KT // 4):
                            load(l, c, (rows(w_up, l, 4 * k, 4, col + u * BLK, BLK), CHUNK, BLK))
                            c += 1
                    return c

                def load_at(l, c, u12, pieces):
                    slot = c % RAW_SLOTS
                    sp.wait_ge(lo_done, 2 * CHUNKS * l + 2 * u12 + 2 * c + 2)
                    sp.sem_inc(slot_seen, 1)
                    src, width, shape = pieces
                    sp.dma_start(raw[:, slot, 0:width].rearrange("p (a b) -> p a b", b=shape),
                                 src).then_inc(raw_landed[slot], 16)

                c = gate_up(l, 0, c)
                with sp.Fori(1, UNITS) as u:
                    u12 = (u - 1) * 12
                    n = c
                    for col in (0, D_FF):
                        for k in range(KT // 4):
                            load_at(l, n, u12, (rows(w_up, l, 4 * k, 4, col + u * BLK, BLK), CHUNK, BLK))
                            n += 1
                    for j in range(N_BLK):
                        load_at(l, n, u12, (rows(w_down, l, (u - 1) * 4, 4, j * BLK, BLK), CHUNK, BLK))
                        n += 1
                c += 12 * (UNITS - 1)
                for j in range(N_BLK):
                    load(l, c, (rows(w_down, l, 4 * (UNITS - 1), 4, j * BLK, BLK), CHUNK, BLK))
                    c += 1
                for i in range(2):
                    load(l, c, (rows(w_ple, l, 0, 2, i * 2 * BLK, 2 * BLK), CHUNK, 2 * BLK))
                    c += 1
                    for j in (2 * i, 2 * i + 1):
                        for k in range(KT // 4):
                            load(l, c, square(w_ple_gate, l, k, j * BLK))
                            c += 1
                assert c == CHUNKS
            for c in range(AHEAD // 2):
                sp.wait_ge(lo_done, 2 * CHUNKS * L + 2 * c + 2)
                sp.sem_inc(raw_landed[c % RAW_SLOTS], 16)
            o_v = out.rearrange("o (t p) n -> p (o t) n", p=P)
            for j in range(N_BLK):
                sp.wait_ge(fin_done, TT * (j + 1))
                sp.dma_start(o_v[:, :, j * BLK:(j + 1) * BLK], h[:, :, j * BLK:(j + 1) * BLK]).then_inc(stored, 16)
            sp.wait_ge(stored, 16 * N_BLK)

        @block.gpsimd
        def _(pool):
            n = [0]
            with nc.allow_non_contiguous_dma(reason="256 positions, once"):
                pool.dma_start(pos_i[:, :], positions.rearrange("o (t p) -> p (o t)", p=P)).then_inc(pos_landed, 16)

            def step(ins):
                n[0] += 1
                ins.then_inc(pool_setup, 1)

            def after():
                pool.wait_ge(pool_setup, n[0])

            step(pool.memset(ident[:, :], 0.0))
            step(pool.memset(mask[:, :], 0.0))
            for i, value in enumerate((1.0 / D, 1.0 / LORA, EPS, -0.5, 0.5)):
                step(pool.memset(consts[:, i, :], value))
            step(pool.iota(inv_cnt[:, :], [[1, 16]], base=1, channel_multiplier=0,
                           allow_small_or_imprecise_dtypes=True))
            after()
            step(pool.affine_select(out=ident[:, :], in_=ident[:, :], compare_op=ALU.not_equal, fill=1.0,
                                    base=0, pattern=[[-1, P]], channel_multiplier=1))
            step(pool.affine_select(out=mask[:, P:2 * P], in_=mask[:, P:2 * P], compare_op=ALU.is_ge,
                                    fill=MASKED, base=0, pattern=[[-1, P]], channel_multiplier=1))
            for i in range(ROPE // 2):
                f = np.float32(1.0) / np.power(np.float32(THETA), np.float32(2 * i) / np.float32(ROPE))
                step(pool.memset(inv_freq[:, i:i + 1], float(f)))
            for g, w in enumerate(POOL_WINDOWS):
                step(pool.memset(band[:, g, :], 1.0 / w))
            after()
            pool.wait_ge(dve_setup, 1)
            for g, w in enumerate(POOL_WINDOWS):
                step(pool.tensor_copy(band[:, g, 0:w], inv_cnt[:, 0:w]))
            after()
            for g, w in enumerate(POOL_WINDOWS):
                for c0, cn in ((0, 2 * P), (2 * P, P)):
                    b = band[:, g, c0:c0 + cn]
                    step(pool.affine_select(out=b, in_=b, compare_op=ALU.is_ge, fill=0.0, base=0,
                                            pattern=[[1, cn]], channel_multiplier=-1))
                    after()
                    step(pool.affine_select(out=b, in_=b, compare_op=ALU.is_ge, fill=0.0, base=w - 1,
                                            pattern=[[-1, cn]], channel_multiplier=1))
            after()
            for g in range(len(POOL_WINDOWS)):
                for c0 in (0, 2 * P):
                    step(pool.tensor_tensor(band[:, g, c0:c0 + P], band[:, g, c0:c0 + P], ident[:, :],
                                            ALU.subtract))
            assert n[0] == POOL_SETUP

            def factor(done, src, dst, n_terms, step0, halved=False):
                k = 0
                pool.wait_ge(rstd_done, done + 1)
                if src.shape[-1] == N_BLK and len(src.shape) == 3:
                    pool.tensor_tensor(part[:, :, :], src[:, :, 0:2], src[:, :, 2:4], ALU.add).then_inc(rstd_step, 1)
                    pool.wait_ge(rstd_step, step0 + 1)
                    pool.tensor_tensor(mean[:, :], part[:, :, 0], part[:, :, 1], ALU.add).then_inc(rstd_step, 1)
                    pool.wait_ge(rstd_step, step0 + 2)
                    k, src = 2, mean[:, :]
                pool.tensor_tensor(mean[:, :], src, consts[:, n_terms, :], ALU.mult).then_inc(rstd_step, 1)
                pool.wait_ge(rstd_step, step0 + k + 1)
                pool.tensor_tensor(mean[:, :], mean[:, :], consts[:, C_EPS, :], ALU.add).then_inc(rstd_step, 1)
                pool.wait_ge(rstd_step, step0 + k + 2)
                ins = pool.tensor_tensor(dst[:, :], mean[:, :], consts[:, C_POWER, :], ALU.pow)
                if halved:
                    ins.then_inc(rstd_step, 1)
                    pool.wait_ge(rstd_step, step0 + k + 3)
                    ins = pool.tensor_tensor(dst[:, :], dst[:, :], consts[:, C_HALF, :], ALU.mult)
                ins.then_inc(rstd_done, 1)

            STEPS = 4 + 2 + 2 + 4 + 5
            p_v = p.rearrange("l o (t p) n -> l p (o t) n", p=P)
            pool.sem_inc(rstd_done, 1)
            with pool.Fori(0, L) as l:
                pool.wait_ge(sq_done, TT * (3 * N_BLK * l + N_BLK))
                factor(5 * l + 0, sumsq[:, :, :], rstd["mix"], C_D, STEPS * l)
                pool.wait_ge(sq_lat_done, 2 * TT * l + TT)
                factor(5 * l + 1, sumsq_lat[:, 0, :], rstd["q"], C_LORA, STEPS * l + 4)
                pool.wait_ge(sq_lat_done, 2 * TT * l + 2 * TT)
                factor(5 * l + 2, sumsq_lat[:, 1, :], rstd["kv"], C_LORA, STEPS * l + 6)
                pool.wait_ge(sq_done, TT * (3 * N_BLK * l + 2 * N_BLK))
                factor(5 * l + 3, sumsq[:, :, :], rstd["ffn"], C_D, STEPS * l + 8)
                pool.wait_ge(t_ready, JOBS * l + JB["ffn"] + 1)
                pool.dma_start(p_tok[:, :, :], p_v[bass.ds(l, 1)].rearrange("l p t n -> p (l t) n")).then_inc(
                    p_landed, 16)
                pool.wait_ge(sq_done, TT * (3 * N_BLK * l + 3 * N_BLK))
                factor(5 * l + 4, sumsq[:, :, :], rstd["ple"], C_D, STEPS * l + 12, halved=True)
            pool.wait_ge(h_ready, 3 * N_BLK * L + N_BLK)
            pool.dma_start(fin_g[:, :], final_norm_g.rearrange("(o n) -> o n", o=1).broadcast_to([P, D])).then_inc(
                fin_landed, 16)
            pool.wait_ge(sq_done, TT * (3 * N_BLK * L + N_BLK))
            factor(5 * L, sumsq[:, :, :], rstd["final"], C_D, STEPS * L)

        @block.scalar
        def _(act):
            copy = nc.scalar.activation

            x_v = x.rearrange("o (t p) n -> p (o t) n", p=P)
            for j in range(N_BLK):
                act.dma_start(h[:, :, j * BLK:(j + 1) * BLK], x_v[:, :, j * BLK:(j + 1) * BLK]).then_inc(
                    x_landed[j], 16)
            for t in range(3):
                act.dma_start(rows_c[t // 2][FKT * (t % 2):FKT * (t % 2 + 1)],
                              conv_w[:, t].rearrange("l (k p) -> k l p", p=P)).then_inc(conv_landed, 16)
            act.dma_start(rows_c[1][FKT:2 * FKT], conv_b.rearrange("l (k p) -> k l p", p=P)).then_inc(conv_landed, 16)
            for c0, g in ((G_Q, q_norm_g), (G_KV, kv_norm_g)):
                act.dma_start(prm_all[:, :, c0:c0 + LKT], g.rearrange("l (p k) -> p l k", k=LKT)).then_inc(
                    lat_landed, 16)
            def split(l, m):
                c = m // 2
                act.wait_ge(raw_landed[c % RAW_SLOTS], l * (CHUNKS // RAW_SLOTS * 16) + (c // RAW_SLOTS * 16 + 16))
                act.wait_ge(w_used, l * (2 * CHUNKS) + m + 1)
                copy(w_hi[:, half_of(m), :], raw[:, c % RAW_SLOTS, (m % 2) * HALF:(m % 2 + 1) * HALF],
                     ACT.Copy).then_inc(hi_done, 1)

            def steps(l, a, b):
                for m in range(a, b):
                    split(l, m + AHEAD)

            for j in range(N_BLK):
                act.wait_ge(x_landed[j], 16)
                act.sem_inc(h_ready, 1)
                for t in range(TT):
                    if j > 0:
                        act.wait_ge(sq_done, TT * (j - 1) + t + 1)
                    copy(sq_setup[:, t, :], h[:, t, j * BLK:(j + 1) * BLK], ACT.Square,
                         accum_out=sumsq[:, t, j:j + 1]).then_inc(sq_done, 1)
                if j == 0:
                    split(0, 0)
                    split(0, 1)
            split(0, 2)
            split(0, 3)
            act.wait_ge(dve_setup, DVE_REDUCED)
            copy(sin[:, :, :], red[:, 0], ACT.Sin).then_inc(act_setup, 1)
            copy(cos[:, :, :], red[:, 1], ACT.Sin).then_inc(act_setup, 1)
            act.wait_ge(pool_setup, POOL_SETUP)
            copy(band_hi[:, :, :], band[:, :, :], ACT.Copy).then_inc(act_setup, 1)

            def gained(l, job, dst, kt, gain, done, value=None):
                act.wait_ge(t_ready, JOBS * l + job + 1)
                for i in range(2):
                    ins = copy(dst[0][:, kt + i, :], tps[:, job % T_BANKS, i * S:(i + 1) * S], ACT.Copy,
                               scale=scalar_of(gain + i))
                ins.then_inc(done, 1)

            def squares(l, j, number):
                act.wait_ge(h_ready, 3 * N_BLK * l + N_BLK + number + 1)
                for t in range(TT):
                    act.wait_ge(sq_done, TT * (3 * N_BLK * l + N_BLK + number - 1) + t + 1)
                    copy(sq_h[:, t, :], h[:, t, j * BLK:(j + 1) * BLK], ACT.Square,
                         accum_out=sumsq[:, t, j:j + 1]).then_inc(sq_done, 1)

            def whole(l, b, bank, dst, done):
                copy(dst, acc[b % 2][:, bank, :], ACT.Copy).then_inc(done, 1)

            with act.Fori(0, L) as l:
                act.wait_ge(prm_ready, l + 1)
                mix_job = lambda i: gained(l, JB["mix"] + i, xa, 2 * i, G_MIX + 2 * i, hT_hi)
                for i in range(4):
                    mix_job(i)
                steps(l, 0, 2)
                for i in range(4, 6):
                    mix_job(i)
                steps(l, 2, 4)
                for i in range(6, 8):
                    mix_job(i)
                steps(l, 4, 8)

                def latent(i):
                    b = BL["cq"] + i
                    block_ready(act, l, b)
                    if i == 0:
                        act.wait_ge(rstd_done, 5 * l + 2)
                    for t in range(TT):
                        copy(lat[:, i, t, :], acc[b % 2][:, t, :], ACT.Copy,
                             scale=rstd["mix"][:, t:t + 1]).then_inc(acc_free[b % 2], 1)
                    for t in range(TT):
                        act.wait_ge(acc_free[b % 2], BLOCKS * l + 2 * (b // 2 + 1) + t + 1)
                        if i == 1:
                            act.wait_ge(sq_lat_done, 2 * TT * l + t + 1)
                        copy(sq_lat[:, t, :], lat[:, i, t, :], ACT.Square,
                             accum_out=sumsq_lat[:, i, t:t + 1]).then_inc(sq_lat_done, 1)

                latent(0)
                steps(l, 8, 12)
                for i in range(2):
                    gained(l, JB["cq"] + i, xb, LAT_Q + 2 * i, G_Q + 2 * i, lat_hi)
                steps(l, 12, 16)
                latent(1)
                steps(l, 16, 18)
                b = BL["kr"]
                block_ready(act, l, b)
                for t in range(TT):
                    ins = copy(kr_in[:, t, :], acc[b % 2][:, t, 0:ROPE], ACT.Copy,
                               scale=rstd["mix"][:, t:t + 1])
                    ins.then_inc(acc_free[b % 2], 1)
                steps(l, 18, 20)
                act.wait_ge(t_ready, JOBS * l + JB["kr"] + 1)
                bank = tps[:, JB["kr"] % T_BANKS, 0:S]
                copy(krt[0][0:ROPE, 0, :], bank[0:ROPE], ACT.Copy)
                copy(krt[0][ROPE:P, 1, :], bank[ROPE:P], ACT.Copy).then_inc(kr_hi, 1)
                for i in range(2):
                    gained(l, JB["ckv"] + i, xb, LAT_KV + 2 * i, G_KV + 2 * i, lat_hi)
                steps(l, 20, 26)

                def pooled(i):
                    b = BL["pool"] + i
                    block_ready(act, l, b)
                    for t in range(TT):
                        copy(up_[0][:, t, :], acc[b % 2][:, t, :], ACT.Copy,
                             scale=rstd["mix"][:, t:t + 1]).then_inc(upool_hi, 1)

                def diffs(i):
                    for k in range(2):
                        job = JB["diff"] + 2 * i + k
                        act.wait_ge(t_ready, JOBS * l + job + 1)
                        kt = DIFF + 4 * i + 2 * k
                        copy(xb[0][:, kt:kt + 2, :].rearrange("p a b -> p (a b)"), tps[:, job % T_BANKS, :],
                             ACT.Copy).then_inc(diff_hi, 1)

                pooled(0)
                steps(l, 26, 28)
                diffs(0)
                steps(l, 28, 34)
                pooled(1)
                steps(l, 34, 38)

                def qk(b, kt, number=None):
                    if number is None:
                        block_ready(act, l, b)
                    else:
                        act.wait_ge(pair_ready, 5 * l + number)
                    for k in range(2):
                        whole(l, b, k, xa[0][:, kt + 2 * k:kt + 2 * k + 2, :].rearrange("p a b -> p (a b)"), qk_hi)

                qk(BL["qnope"], Q_T, 1)
                qk(BL["qnope"] + 1, Q_T + 4)
                steps(l, 38, 40)
                diffs(1)
                steps(l, 40, 42)
                qk(BL["knope"], K_T, 2)
                qk(BL["knope"] + 1, K_T + 4)
                steps(l, 42, 44)
                for i in range(2):
                    job = JB["qrope"] + i
                    act.wait_ge(t_ready, JOBS * l + job + 1)
                    copy(qrt[0][:, 2 * i:2 * i + 2, :].rearrange("p a b -> p (a b)"), tps[:, job % T_BANKS, :],
                         ACT.Copy).then_inc(qr_hi, 1)
                steps(l, 44, 46)
                for i in range(2):
                    b = BL["v"] + i
                    if i == 0:
                        act.wait_ge(pair_ready, 5 * l + 3)
                    else:
                        block_ready(act, l, b)
                    for t in range(TT):
                        whole(l, b, t, v[0][:, t, i * BLK:(i + 1) * BLK], v_hi)
                steps(l, 46, 48)

                for i in range(HEADS + 2):
                    if i == HEADS + 1:
                        steps(l, 50 + i, 51 + i)
                    if i >= 2:
                        act.wait_ge(t_ready, JOBS * l + JY[i - 2] + 1)
                        copy(xb[0][:, PKT + i - 2, :], tps[:, JY[i - 2] % T_BANKS, 0:S], ACT.Copy).then_inc(y_hi, 1)
                    if 1 <= i <= HEADS:
                        act.wait_ge(t_ready, JOBS * l + JT[i - 1] + 1)
                        copy(pt[0][:, :], tps[:, JT[i - 1] % T_BANKS, 0:3 * P], ACT.Copy).then_inc(pt_hi, 1)
                    if i < HEADS:
                        act.wait_ge(s_ready, HEADS * l + i + 1)
                        copy(prob[:, i % 2, 0:P], prob[:, i % 2, 0:P], ACT.Exp, bias=nmx[:, i % 2, 0:1],
                             scale=SCALE, accum_out=psums[:, i % 2, 0:1])
                        copy(prob[:, i % 2, P:3 * P], prob[:, i % 2, P:3 * P], ACT.Exp, bias=nmx[:, i % 2, 1:2],
                             scale=SCALE, accum_out=psums[:, i % 2, 1:2]).then_inc(e_done, 1)
                    if i in (1, 2):
                        b = BL["poolw"] + i - 1
                        block_ready(act, l, b)
                        for k in range(4):
                            kt = 4 * (i - 1) + k
                            copy(xb[0][:, kt, :], acc[b % 2][:, k // 2, (k % 2) * S:(k % 2 + 1) * S], ACT.Copy,
                                 scale=scalar_of(POOL_S + kt)).then_inc(ypool_hi, 1)
                    if i < 2:
                        steps(l, 48 + 2 * i, 50 + 2 * i)
                    elif i <= HEADS:
                        steps(l, 50 + i, 51 + i)

                def norm_job(job0, i, dst, gain):
                    gained(l, job0 + i, dst, 2 * i, gain + 2 * i, hT_hi)

                def out_job(j):
                    for i in (2 * j, 2 * j + 1):
                        norm_job(JB["ffn_norm"], i, xa, G_FFN)

                steps(l, 60, 66)
                squares(l, 0, 0)
                out_job(0)
                steps(l, 66, 70)
                squares(l, 1, 1)
                out_job(1)
                steps(l, 70, 78)
                squares(l, 2, 2)
                out_job(2)
                steps(l, 78, 86)
                squares(l, 3, 3)
                out_job(3)

                def split_u(l, v, m):
                    c = m // 2
                    act.wait_ge(raw_landed[c % RAW_SLOTS],
                                l * (CHUNKS // RAW_SLOTS * 16) + v * (12 // RAW_SLOTS * 16)
                                + (c // RAW_SLOTS * 16 + 16))
                    act.wait_ge(w_used, l * (2 * CHUNKS) + v * 24 + (m + 1))
                    copy(w_hi[:, half_of(m), :], raw[:, c % RAW_SLOTS, (m % 2) * HALF:(m % 2 + 1) * HALF],
                         ACT.Copy).then_inc(hi_done, 1)

                def unit(l, u, v, with_down, done_before):
                    m0 = 2 * CH["ffn"] + (16 if with_down else 0)
                    b0 = BL["ffn"] + (2 if with_down else 0)

                    def go(a, b):
                        for m in range(a, b):
                            split_u(l, v, m0 + m + AHEAD)

                    def at_block(k):
                        block_ready(act, l, b0 + k, v)

                    def rows_out(k, dst):
                        at_block(k)
                        for t in range(TT):
                            copy(dst[:, t, :], acc[(b0 + k) % 2][:, t, :], ACT.Copy,
                                 scale=rstd["ffn"][:, t:t + 1]).then_inc(acc_free[(b0 + k) % 2], 1)

                    go(done_before, 8)
                    if not with_down:
                        act.wait_ge(rstd_done, 5 * l + 5)
                    rows_out(0, gate_tok)
                    go(8, 13)
                    act.wait_ge(conv_done, UNITS * l + u + 1)
                    copy(sig[:, :, :], conv[:, :, :], ACT.Tanh, scale=0.5).then_inc(tanh_done, 1)
                    go(13, 16)
                    rows_out(1, up_tok)
                    if with_down:
                        go(16, 24)
                        at_block(1 + N_BLK)
                    act.wait_ge(g_done, UNITS * l + u + 1)
                    copy(gt[0][:, :, :], conv[:, :, :], ACT.Copy).then_inc(g_hi, 1)

                unit(l, 0, 0, False, 2)
                with act.Fori(1, UNITS) as u:
                    unit(l, u, u - 1, True, 0)

                d0 = 2 * (CHUNKS - plan["n_blk"] * 4 - 2 - N_BLK)

                def ple_job(j):
                    for i in (2 * j, 2 * j + 1):
                        norm_job(JB["ple_norm"], i, xb, G_PLE)

                steps(l, d0, d0 + 1)
                act.wait_ge(t_ready, JOBS * l + JB["p"] + 1)
                copy(ppt[0][:, :, :].rearrange("p a b -> p (a b)"), tps[:, JB["p"] % T_BANKS, :], ACT.Copy).then_inc(
                    p_hi, 1)
                steps(l, d0 + 1, d0 + 3)
                e0 = d0 + 2 * N_BLK

                def pw_out(i):
                    for k in range(2):
                        b = BL["ple"] + 4 * i + k
                        if k == 0:
                            act.wait_ge(pair_ready, 5 * l + 4 + i)
                        else:
                            block_ready(act, l, b)
                        for t in range(TT):
                            copy(pw[:, i, t, k * BLK:(k + 1) * BLK], acc[b % 2][:, t, :], ACT.Copy).then_inc(
                                acc_free[b % 2], 1)

                def gate_tanh(j):
                    b = BL["ple"] + 2 + j + 2 * (j // 2)
                    block_ready(act, l, b)
                    if j == 0:
                        act.wait_ge(rstd_done, 5 * l + 6)
                    if j >= 2:
                        act.wait_ge(h_ready, 3 * N_BLK * l + N_BLK + 2 * N_BLK + j - 1)
                    for t in range(TT):
                        copy(sg[:, j % 2, t, :], acc[b % 2][:, t, :], ACT.Tanh,
                             scale=rstd["ple"][:, t:t + 1]).then_inc(acc_free[b % 2], 1)

                for j in range(N_BLK - 1):
                    squares(l, j, N_BLK + j)
                    ple_job(j)
                    steps(l, d0 + 3 + 2 * j, d0 + 5 + 2 * j)
                squares(l, 3, N_BLK + 3)
                steps(l, d0 + 9, e0 + 2)
                pw_out(0)
                ple_job(3)
                steps(l, e0 + 2, e0 + 12)
                gate_tanh(0)
                steps(l, e0 + 12, e0 + 14)
                squares(l, 0, 2 * N_BLK)
                steps(l, e0 + 14, e0 + 20)
                gate_tanh(1)
                pw_out(1)
                squares(l, 1, 2 * N_BLK + 1)
                steps(l, e0 + 20, e0 + 30)
                gate_tanh(2)
                steps(l, e0 + 30, e0 + 32)
                squares(l, 2, 2 * N_BLK + 2)
                steps(l, e0 + 32, e0 + 36)
                gate_tanh(3)
                squares(l, 3, 2 * N_BLK + 3)

        @block.vector
        def _(dve):
            n = [0]

            def step(ins):
                n[0] += 1
                ins.then_inc(dve_setup, 1)

            def after():
                dve.wait_ge(dve_setup, n[0])

            dve.sem_inc(lo_done, HALF_SLOTS)
            for i in range(2):
                dve.sem_inc(acc_free[i], 2)
            dve.wait_ge(pool_setup, 8)
            step(dve.reciprocal(inv_cnt[:, :], inv_cnt[:, :]))
            for i in range(2):
                step(dve.memset(krt[i][ROPE:P, 0, :].bitcast(F32), 0.0))
                step(dve.memset(krt[i][0:ROPE, 1, :].bitcast(F32), 0.0))
            dve.wait_ge(pos_landed, 16)
            step(dve.tensor_copy(pos_f[:, :], pos_i[:, :]))
            after()
            dve.wait_ge(pool_setup, 10 + ROPE // 2)
            for t in range(TT):
                step(dve.tensor_scalar(ang[:, t, :], inv_freq[:, :], pos_f[:, t:t + 1], None, ALU.mult))
            after()
            for i in range(2):
                step(dve.tensor_scalar(turns[:, i], ang[:, :, :], float(1.0 / (2.0 * np.pi)), 0.25 * i, ALU.mult,
                                       ALU.add))
            after()
            magic = 1.5 * 2.0 ** 23
            step(dve.tensor_scalar(turns[:, :], turns[:, :], magic, None, ALU.add))
            after()
            step(dve.tensor_scalar(turns[:, :], turns[:, :], magic, None, ALU.subtract))
            after()
            parts = [6.28125]
            parts.append(float(np.float32(np.float64(2 * np.pi - parts[0]) // 2.0 ** -20 * 2.0 ** -20)))
            parts.append(float(np.float32(2 * np.pi - parts[0] - parts[1])))
            for i in range(2):
                step(dve.scalar_tensor_tensor(red[:, i], turns[:, i], -parts[0], ang[:, :, :], ALU.mult, ALU.add))
            after()
            for c in parts[1:]:
                step(dve.scalar_tensor_tensor(red[:, :], turns[:, :], -c, red[:, :], ALU.mult, ALU.add))
                after()
            step(dve.tensor_scalar(red[:, 1], red[:, 1], float(np.pi / 2), None, ALU.add))
            after()
            step(dve.tensor_scalar(red[:, :], red[:, :], 3.1415925, -3.1415925, ALU.min, ALU.max))
            assert n[0] == DVE_REDUCED
            for l in range(L):
                dve.wait_ge(prm_t, l + 1)
                step(dve.tensor_copy(prm_all[:, l, 0:G_Q], tps[:, l, 0:G_Q]))
            dve.wait_ge(act_setup, 3)
            step(dve.tensor_tensor(band_lo[:, :, :], band[:, :, 0:16], band_hi[:, :, 0:16].bitcast(F32),
                                   ALU.subtract))
            dve.wait_ge(lat_landed, 16 * 2)
            after()
            dve.sem_inc(t_done, T_BANKS)

            def split(l, m, v=None):
                c = m // 2
                if v is None:
                    base = l * (2 * CHUNKS)
                else:
                    base = l * (2 * CHUNKS) + v * 24
                dve.wait_ge(hi_done, base + (m + 1))
                dve.wait_ge(w_used, base + (m + 1))
                dve.tensor_tensor(w_lo[:, half_of(m), :], raw[:, c % RAW_SLOTS, (m % 2) * HALF:(m % 2 + 1) * HALF],
                                  w_hi[:, half_of(m), :].bitcast(F32), ALU.subtract).then_inc(lo_done, 1)

            def steps(l, a, b):
                for m in range(a, b):
                    split(l, m + AHEAD)

            for m in range(AHEAD):
                split(0, m)

            def lo(dst, src, hi, gain=None):
                if gain is None:
                    return dve.tensor_tensor(dst, src, hi.bitcast(F32), ALU.subtract)
                return dve.scalar_tensor_tensor(dst, src, gain, hi.bitcast(F32), ALU.mult, ALU.subtract)

            def gained(l, job, dst, kt, gain, hi_sem, value):
                dve.wait_ge(hi_sem, value)
                for i in range(2):
                    ins = lo(dst[1][:, kt + i, :], tps[:, job % T_BANKS, i * S:(i + 1) * S], dst[0][:, kt + i, :],
                             scalar_of(gain + i))
                ins.then_inc(t_done, 1)

            with dve.Fori(0, L) as l:
                dve.tensor_copy(prm[:, :], prm_all[:, bass.ds(l, 1), :].rearrange("p a b -> p (a b)")).then_inc(
                    prm_ready, 1)
                dve.wait_ge(prm_ready, l + 1)
                mix_job = lambda i: gained(l, JB["mix"] + i, xa, 2 * i, G_MIX + 2 * i, hT_hi, 3 * HJ * l + i + 1)
                for i in range(4):
                    mix_job(i)
                steps(l, 0, 2)
                for i in range(4, 6):
                    mix_job(i)
                steps(l, 2, 4)
                for i in range(6, 8):
                    mix_job(i)
                steps(l, 4, 10)

                def latent(i):
                    dve.wait_ge(rstd_done, 5 * l + 3 + i)
                    for t in range(TT):
                        ins = dve.tensor_scalar(lat[:, i, t, :], lat[:, i, t, :],
                                                rstd[("q", "kv")[i]][:, t:t + 1], None, ALU.mult)
                    ins.then_inc(lat_norm, 1)

                latent(0)
                steps(l, 10, 12)
                for i in range(2):
                    gained(l, JB["cq"] + i, xb, LAT_Q + 2 * i, G_Q + 2 * i, lat_hi, 4 * l + i + 1)
                steps(l, 12, 18)
                latent(1)

                dve.wait_ge(acc_free[BL["kr"] % 2], BLOCKS * l + 2 * (BL["kr"] // 2 + 2))
                half = ROPE // 2
                x1, x2 = kr_in[:, :, 0:half], kr_in[:, :, half:ROPE]
                o1, o2 = kr_tok[:, :, 0:half], kr_tok[:, :, half:ROPE]
                dve.tensor_tensor(o1, x1, cos[:, :, :], ALU.mult)
                dve.tensor_tensor(kr_tmp[:, 0], x2, sin[:, :, :], ALU.mult)
                dve.tensor_tensor(o2, x2, cos[:, :, :], ALU.mult)
                dve.tensor_tensor(kr_tmp[:, 1], x1, sin[:, :, :], ALU.mult).then_inc(kr_step, 1)
                dve.wait_ge(kr_step, 3 * l + 1)
                dve.tensor_tensor(o1, o1, kr_tmp[:, 0], ALU.subtract)
                dve.tensor_tensor(o2, o2, kr_tmp[:, 1], ALU.add).then_inc(kr_step, 1)
                dve.wait_ge(kr_step, 3 * l + 2)
                dve.tensor_copy(kr_tok[:, :, ROPE:P], kr_tok[:, :, 0:ROPE]).then_inc(kr_step, 1)
                steps(l, 18, 20)
                dve.wait_ge(kr_hi, l + 1)
                bank = tps[:, JB["kr"] % T_BANKS, 0:S]
                lo(krt[1][0:ROPE, 0, :], bank[0:ROPE], krt[0][0:ROPE, 0, :])
                lo(krt[1][ROPE:P, 1, :], bank[ROPE:P], krt[0][ROPE:P, 1, :]).then_inc(t_done, 1)
                for i in range(2):
                    gained(l, JB["ckv"] + i, xb, LAT_KV + 2 * i, G_KV + 2 * i, lat_hi, 4 * l + 3 + i)
                steps(l, 20, 26)

                def pooled(i):
                    b = BL["pool"] + i
                    for t in range(TT):
                        dve.wait_ge(upool_hi, 2 * TT * l + TT * i + t + 1)
                        lo(up_[1][:, t, :], acc[b % 2][:, t, :], up_[0][:, t, :],
                           rstd["mix"][:, t:t + 1]).then_inc(acc_free[b % 2], 1)

                def diffs(i):
                    for k in range(2):
                        job = JB["diff"] + 2 * i + k
                        dve.wait_ge(diff_hi, 4 * l + 2 * i + k + 1)
                        kt = DIFF + 4 * i + 2 * k
                        two = lambda x: x[:, kt:kt + 2, :].rearrange("p a b -> p (a b)")
                        lo(two(xb[1]), tps[:, job % T_BANKS, :], two(xb[0])).then_inc(t_done, 1)

                pooled(0)
                steps(l, 26, 28)
                diffs(0)
                steps(l, 28, 34)
                pooled(1)
                steps(l, 34, 36)

                b = BL["qrope"]
                block_ready(dve, l, b)
                for t in range(TT):
                    q = acc[b % 2][:, t, :].rearrange("p (h c) -> p h c", c=ROPE)
                    o = qr_tok[:, t, :].rearrange("p (h c) -> p h c", c=ROPE)
                    tmp = [qr_tmp[:, i, :].rearrange("p (h c) -> p h c", c=half) for i in range(2)]
                    ct, st = (z[:, t, :].unsqueeze(1).broadcast_to([P, HEADS, half]) for z in (cos, sin))
                    q1, q2 = q[:, :, 0:half], q[:, :, half:ROPE]
                    o1, o2 = o[:, :, 0:half], o[:, :, half:ROPE]
                    dve.tensor_tensor(o1, q1, ct, ALU.mult)
                    dve.tensor_tensor(tmp[0], q2, st, ALU.mult).then_inc(qr_step, 1)
                    dve.tensor_tensor(o2, q2, ct, ALU.mult)
                    dve.tensor_tensor(tmp[1], q1, st, ALU.mult).then_inc(acc_free[b % 2], 1)
                    dve.wait_ge(qr_step, 3 * TT * l + 3 * t + 1)
                    dve.tensor_tensor(o1, o1, tmp[0], ALU.subtract).then_inc(qr_step, 1)
                    dve.wait_ge(acc_free[b % 2], BLOCKS * l + 2 * (b // 2 + 1) + t + 1)
                    dve.tensor_tensor(o2, o2, tmp[1], ALU.add).then_inc(qr_step, 1)
                    dve.wait_ge(qr_step, 3 * TT * l + 3 * t + 3)
                steps(l, 36, 38)

                def qk(b, kt, number):
                    for k in range(2):
                        dve.wait_ge(qk_hi, 8 * l + number + k + 1)
                        two = lambda x: x[:, kt + 2 * k:kt + 2 * k + 2, :].rearrange("p a b -> p (a b)")
                        lo(two(xa[1]), acc[b % 2][:, k, :], two(xa[0])).then_inc(acc_free[b % 2], 1)

                qk(BL["qnope"], Q_T, 0)
                qk(BL["qnope"] + 1, Q_T + 4, 2)
                steps(l, 38, 40)
                diffs(1)
                steps(l, 40, 42)
                qk(BL["knope"], K_T, 4)
                qk(BL["knope"] + 1, K_T + 4, 6)
                steps(l, 42, 44)
                for i in range(2):
                    job = JB["qrope"] + i
                    dve.wait_ge(qr_hi, 2 * l + i + 1)
                    two = lambda x: x[:, 2 * i:2 * i + 2, :].rearrange("p a b -> p (a b)")
                    lo(two(qrt[1]), tps[:, job % T_BANKS, :], two(qrt[0])).then_inc(t_done, 1)
                steps(l, 44, 46)
                for i in range(2):
                    b = BL["v"] + i
                    for t in range(TT):
                        dve.wait_ge(v_hi, 4 * l + 2 * i + t + 1)
                        lo(v[1][:, t, i * BLK:(i + 1) * BLK], acc[b % 2][:, t, :],
                           v[0][:, t, i * BLK:(i + 1) * BLK]).then_inc(acc_free[b % 2], 1)
                steps(l, 46, 48)

                for i in range(HEADS + 2):
                    k = i % 2
                    if i < HEADS:
                        bank = tps[:, JS[i] % T_BANKS]
                        dve.wait_ge(t_ready, JOBS * l + JS[i] + 1)
                        dve.sem_inc(scores_seen, 1)
                        dve.tensor_tensor_reduce(prob[:, k, 0:P], bank[:, 0:P], mask[:, P:2 * P], 1.0, MASKED,
                                                 ALU.add, ALU.max, mx[:, k, 0:1])
                        dve.tensor_tensor_reduce(prob[:, k, P:3 * P], bank[:, P:3 * P], mask[:, :], 1.0, MASKED,
                                                 ALU.add, ALU.max, mx[:, k, 1:2]).then_inc(t_done, 1)
                        dve.wait_ge(t_done, JOBS * l + JS[i] + 1 + T_BANKS)
                        dve.tensor_scalar(nmx[:, k, :], mx[:, k, :], -SCALE, None, ALU.mult).then_inc(s_ready, 1)
                    if i == HEADS + 1:
                        steps(l, 50 + i, 51 + i)
                    if i >= 2:
                        dve.wait_ge(y_hi, HEADS * l + i - 1)
                        lo(xb[1][:, PKT + i - 2, :], tps[:, JY[i - 2] % T_BANKS, 0:S],
                           xb[0][:, PKT + i - 2, :]).then_inc(t_done, 1)
                    if 1 <= i <= HEADS:
                        dve.wait_ge(pt_hi, HEADS * l + i)
                        lo(pt[1][:, :], tps[:, JT[i - 1] % T_BANKS, 0:3 * P], pt[0][:, :]).then_inc(t_done, 1)
                    if i < HEADS:
                        dve.wait_ge(e_done, HEADS * l + i + 1)
                        dve.reciprocal(prec[:, k, :], psums[:, k, :]).then_inc(p_rec, 1)
                        dve.wait_ge(p_rec, HEADS * l + i + 1)
                        dve.tensor_scalar(prob[:, k, 0:P], prob[:, k, 0:P], prec[:, k, 0:1], None, ALU.mult)
                        dve.tensor_scalar(prob[:, k, P:3 * P], prob[:, k, P:3 * P], prec[:, k, 1:2], None,
                                          ALU.mult).then_inc(p_norm, 1)
                    if i in (1, 2):
                        b = BL["poolw"] + i - 1
                        for k4 in range(4):
                            kt = 4 * (i - 1) + k4
                            if k4 % 2 == 0:
                                dve.wait_ge(ypool_hi, PKT * l + kt + 2)
                            ins = lo(xb[1][:, kt, :], acc[b % 2][:, k4 // 2, (k4 % 2) * S:(k4 % 2 + 1) * S],
                                     xb[0][:, kt, :], scalar_of(POOL_S + kt))
                            if k4 % 2:
                                ins.then_inc(acc_free[b % 2], 1)
                    if i < 2:
                        steps(l, 48 + 2 * i, 50 + 2 * i)
                    elif i <= HEADS:
                        steps(l, 50 + i, 51 + i)

                def add_block(l, b, j, v, finished):
                    block_ready(dve, l, b, v)
                    for t in range(TT):
                        hb = h[:, t, j * BLK:(j + 1) * BLK]
                        dve.tensor_tensor(hb, acc[b % 2][:, t, :], hb, ALU.add).then_inc(acc_free[b % 2], 1)
                    if finished:
                        dve.wait_ge(acc_free[b % 2], BLOCKS * l + 2 * (b // 2 + 2))
                        dve.sem_inc(h_ready, 1)

                def out_job(j):
                    for i in (2 * j, 2 * j + 1):
                        gained(l, JB["ffn_norm"] + i, xa, 2 * i, G_FFN + 2 * i, hT_hi, 3 * HJ * l + HJ + i + 1)

                steps(l, 60, 64)
                add_block(l, BL["out"], 0, None, True)
                steps(l, 64, 66)
                out_job(0)
                steps(l, 66, 68)
                add_block(l, BL["out"] + 1, 1, None, True)
                steps(l, 68, 70)
                out_job(1)
                steps(l, 70, 76)
                add_block(l, BL["out"] + 2, 2, None, True)
                steps(l, 76, 78)
                out_job(2)
                steps(l, 78, 84)
                add_block(l, BL["out"] + 3, 3, None, True)
                steps(l, 84, 86)
                out_job(3)

                def unit(l, u, vv, with_down, done_before):
                    m0 = 2 * CH["ffn"] + (16 if with_down else 0)
                    b0 = BL["ffn"] + (2 if with_down else 0)
                    j0 = JB["ffn"] + (4 if with_down else 0)
                    c0 = 8 * UNITS * l + 8 * u

                    def go(a, b):
                        for m in range(a, b):
                            split(l, m0 + m + AHEAD, vv)

                    def job_ready(k):
                        dve.wait_ge(t_ready, JOBS * l + 4 * vv + (j0 + k + 1))

                    def tap(t, ft):
                        return prm[:, bass.ds(4 * u + (TAP[t] + ft), 1)]

                    def gate_t(ft):
                        return tps[:, (j0 + ft // 2) % T_BANKS, (ft % 2) * S:(ft % 2 + 1) * S]

                    go(done_before, 11)
                    for ft in range(4):
                        if ft % 2 == 0:
                            job_ready(ft // 2)
                        dve.tensor_scalar(conv[:, ft, :], gate_t(ft), tap(2, ft),
                                          prm[:, bass.ds(4 * u + (BIAS + ft), 1)], ALU.mult,
                                          ALU.add).then_inc(conv_step, 1)
                    for ft in range(4):
                        dve.wait_ge(conv_step, c0 + (ft + 1))
                        dve.scalar_tensor_tensor(conv[:, ft, 1:S], gate_t(ft)[:, 0:S - 1], tap(1, ft), conv[:, ft, 1:S],
                                                 ALU.mult, ALU.add).then_inc(conv_step, 1)
                    for ft in range(4):
                        dve.wait_ge(conv_step, c0 + (4 + ft + 1))
                        ins = dve.scalar_tensor_tensor(conv[:, ft, 2:S], gate_t(ft)[:, 0:S - 2], tap(0, ft),
                                                       conv[:, ft, 2:S], ALU.mult, ALU.add)
                        if ft % 2:
                            ins.then_inc(t_done, 1)
                    dve.wait_ge(t_done, JOBS * l + 4 * vv + (j0 + 2 + T_BANKS))
                    dve.sem_inc(conv_done, 1)
                    go(11, 14)
                    dve.wait_ge(tanh_done, UNITS * l + u + 1)
                    dve.scalar_tensor_tensor(conv[:, :, :], sig[:, :, :], 1.0, conv[:, :, :], ALU.add,
                                             ALU.mult).then_inc(silu_done, 1)
                    go(14, 16)

                    def gated():
                        dve.wait_ge(silu_done, UNITS * l + u + 1)
                        for k in range(2):
                            job_ready(2 + k)
                            two = conv[:, 2 * k:2 * k + 2, :].rearrange("p a b -> p (a b)")
                            dve.scalar_tensor_tensor(two, tps[:, (j0 + 2 + k) % T_BANKS, :], 0.5, two, ALU.mult,
                                                     ALU.mult).then_inc(t_done, 1)
                        dve.wait_ge(t_done, JOBS * l + 4 * vv + (j0 + 4 + T_BANKS))
                        dve.sem_inc(g_done, 1)

                    if with_down:
                        go(16, 19)
                        add_block(l, b0 + 2, 0, vv, False)
                        gated()
                        go(19, 21)
                        add_block(l, b0 + 3, 1, vv, False)
                        go(21, 23)
                        add_block(l, b0 + 4, 2, vv, False)
                        go(23, 24)
                        add_block(l, b0 + 5, 3, vv, False)
                    else:
                        gated()
                    dve.wait_ge(g_hi, UNITS * l + u + 1)
                    lo(gt[1][:, :, :], conv[:, :, :], gt[0][:, :, :]).then_inc(g_lo, 1)

                unit(l, 0, 0, False, 2)
                with dve.Fori(1, UNITS) as u:
                    unit(l, u, u - 1, True, 0)

                d0 = 2 * (CHUNKS - 4 * N_BLK - 2 - N_BLK)
                e0 = d0 + 2 * N_BLK
                bd = BL["ple"] - N_BLK

                def ple_job(j):
                    for i in (2 * j, 2 * j + 1):
                        gained(l, JB["ple_norm"] + i, xb, 2 * i, G_PLE + 2 * i, hT_hi, 3 * HJ * l + 2 * HJ + i + 1)

                steps(l, d0, d0 + 1)
                dve.wait_ge(p_hi, l + 1)
                two = lambda x: x[:, :, :].rearrange("p a b -> p (a b)")
                lo(two(ppt[1]), tps[:, JB["p"] % T_BANKS, :], two(ppt[0])).then_inc(t_done, 1)
                steps(l, d0 + 1, d0 + 2)
                for j in range(N_BLK):
                    add_block(l, bd + j, j, None, True)
                    steps(l, d0 + 2 + 2 * j, d0 + 3 + 2 * j)
                    ple_job(j)
                    steps(l, d0 + 3 + 2 * j, d0 + 4 + 2 * j)

                def gate(j):
                    b = BL["ple"] + 2 + j + 2 * (j // 2)
                    dve.wait_ge(acc_free[b % 2], BLOCKS * l + 2 * (b // 2 + 2))
                    if j % 2 == 0:
                        bp = BL["ple"] + 4 * (j // 2) + 1
                        dve.wait_ge(acc_free[bp % 2], BLOCKS * l + 2 * (bp // 2 + 2))
                    pj = slice((j % 2) * BLK, (j % 2 + 1) * BLK)
                    for t in range(TT):
                        sgt = sg[:, j % 2, t, :]
                        dve.scalar_tensor_tensor(sgt, sgt, 1.0, pw[:, j // 2, t, pj], ALU.add,
                                                 ALU.mult).then_inc(ple_step, 1)
                    for t in range(TT):
                        hb = h[:, t, j * BLK:(j + 1) * BLK]
                        dve.wait_ge(ple_step, TT * N_BLK * l + TT * j + t + 1)
                        ins = dve.scalar_tensor_tensor(hb, sg[:, j % 2, t, :], 0.5, hb, ALU.mult, ALU.add)
                    ins.then_inc(h_ready, 1)

                steps(l, e0 + 2, e0 + 12)
                gate(0)
                steps(l, e0 + 12, e0 + 20)
                gate(1)
                steps(l, e0 + 20, e0 + 30)
                gate(2)
                steps(l, e0 + 30, e0 + 36)
                gate(3)

            dve.wait_ge(fin_landed, 16)
            dve.wait_ge(rstd_done, 5 * L + 2)
            dve.wait_ge(h_ready, 3 * N_BLK * L + N_BLK)
            for j in range(N_BLK):
                for t in range(TT):
                    hb = h[:, t, j * BLK:(j + 1) * BLK]
                    dve.scalar_tensor_tensor(hb, hb, rstd["final"][:, t:t + 1], fin_g[:, j * BLK:(j + 1) * BLK],
                                             ALU.mult, ALU.mult).then_inc(fin_done, 1)

        @block.tensor
        def _(pe):
            pe.sem_inc(w_used, HALF_SLOTS)
            pe.wait_ge(rows_landed, 16 * 4)
            pe.wait_ge(pool_setup, 9)
            for l in range(L):
                pe.transpose(tps[:, l, 0:ROWS_G], rows_g[:, l, :], ident[0:ROWS_G, 0:ROWS_G])
            pe.wait_ge(conv_landed, 16 * 4)
            for l in range(L):
                pe.transpose(tps[:, l, TAP[0]:TAP[2]], rows_c[0][:, l, :], ident[0:2 * FKT, 0:2 * FKT])
                pe.transpose(tps[:, l, TAP[2]:G_Q], rows_c[1][:, l, :], ident[0:2 * FKT, 0:2 * FKT]).then_inc(prm_t, 1)

            def three(dst, a_hi, a_lo, b_hi, b_lo, first, last):
                pe.matmul(dst, a_hi, b_hi, start=first, stop=False)
                pe.matmul(dst, a_lo, b_hi, start=False, stop=False)
                return pe.matmul(dst, a_hi, b_lo, start=False, stop=last)

            def halves(l, m, v=None):
                base = l * (2 * CHUNKS) + (HALF_SLOTS + m + 1) if v is None else \
                    l * (2 * CHUNKS) + v * 24 + (HALF_SLOTS + m + 1)
                pe.wait_ge(lo_done, base)
                return w_hi[:, half_of(m), :], w_lo[:, half_of(m), :]

            def free_acc(l, b, v=None):
                if v is None:
                    pe.wait_ge(acc_free[b % 2], BLOCKS * l + 2 * (b // 2 + 1))
                else:
                    pe.wait_ge(acc_free[b % 2], BLOCKS * l + (2 + N_BLK) * v + 2 * (b // 2 + 1))

            def square_half(l, m, b, x, kt, first, last, v=None):
                hi, lo = halves(l, m, v)
                if first:
                    free_acc(l, b, v)
                for k in range(2):
                    cols = slice(k * BLK, (k + 1) * BLK)
                    for t in range(TT):
                        tok = slice(t * P, (t + 1) * P)
                        ins = three(acc[b % 2][:, t, :], x[0][:, kt + k, tok], x[1][:, kt + k, tok], hi[:, cols],
                                    lo[:, cols], first and k == 0, last and k == 1)
                ins.then_inc(w_used, 1)

            def square_halves(l, m, b, x, a, z, v=None):
                for i in range(a, z):
                    square_half(l, m + i, b, x, 2 * i, i == 0, i == KT // 2 - 1, v)

            def new_job(l, job, v=None):
                pe.wait_ge(t_done, JOBS * l + (job + 1) if v is None else JOBS * l + 4 * v + (job + 1))
                return tps[:, job % T_BANKS]

            def jobs_split(l, job, v=None):
                pe.wait_ge(t_done, JOBS * l + (job + 1 + T_BANKS))

            def block_split(l, b, v=None):
                if v is None:
                    pe.wait_ge(acc_free[b % 2], BLOCKS * l + 2 * (b // 2 + 2))
                else:
                    pe.wait_ge(acc_free[b % 2], BLOCKS * l + (2 + N_BLK) * v + 2 * (b // 2 + 2))

            def turn(l, job, tiles, v=None):
                bank = new_job(l, job, v)
                for t in range(TT):
                    for i in range(2):
                        ins = pe.transpose(bank[:, i * S + t * P:i * S + (t + 1) * P], tiles(t, i), ident[:, :])
                ins.then_inc(t_ready, 1)

            def turn_h(l, job0, i):
                turn(l, job0 + i, lambda t, k: h[:, t, (2 * i + k) * P:(2 * i + k + 1) * P])

            with pe.Fori(0, L) as l:
                for i in range(4):
                    if i % 2 == 0:
                        pe.wait_ge(h_ready, 3 * N_BLK * l + i // 2 + 1)
                    turn_h(l, JB["mix"], i)
                m, b = 0, BL["cq"]
                for i in range(4):
                    jobs_split(l, JB["mix"] + 2 * i + 1)
                    square_halves(l, m, b, xa, 2 * i, 2 * i + 2)
                    if i < 2:
                        pe.wait_ge(h_ready, 3 * N_BLK * l + i + 3)
                        turn_h(l, JB["mix"], 4 + 2 * i)
                        turn_h(l, JB["mix"], 5 + 2 * i)
                m, b = 8, BL["ckv"]
                square_halves(l, m, b, xa, 0, 4)

                def turn_lat(i, job):
                    pe.wait_ge(lat_norm, 2 * l + i + 1)
                    for k in range(2):
                        turn(l, job + k, lambda t, n: lat[:, i, t, :].rearrange("p (f k) -> p f k", k=LKT)[
                            :, :, 2 * k + n])

                turn_lat(0, JB["cq"])
                square_halves(l, m, b, xa, 4, 8)
                m, b = 2 * CH["kr"], BL["kr"]
                hi, lo = halves(l, m)
                free_acc(l, b)
                for t in range(TT):
                    tok = slice(t * P, (t + 1) * P)
                    for k in range(KT):
                        cols = slice(k * ROPE, (k + 1) * ROPE)
                        ins = three(acc[b % 2][:, t, 0:ROPE], xa[0][:, k, tok], xa[1][:, k, tok], hi[:, cols],
                                    lo[:, cols], k == 0, k == KT - 1)
                ins.then_inc(w_used, 2)
                m, b = 2 * CH["pool"], BL["pool"]
                square_halves(l, m, b, xa, 0, 2)
                pe.wait_ge(kr_step, 3 * l + 3)
                bank = new_job(l, JB["kr"])
                for t in range(TT):
                    ins = pe.transpose(bank[:, t * P:(t + 1) * P], kr_tok[:, t, :], ident[:, :])
                ins.then_inc(t_ready, 1)
                turn_lat(1, JB["ckv"])
                square_halves(l, m, b, xa, 2, 8)

                def diffs(i):
                    block_split(l, BL["pool"] + i)
                    for k in range(2):
                        g = 2 * i + k
                        job = JB["diff"] + g
                        bank = new_job(l, job)
                        for n in range(2):
                            f = slice((2 * k + n) * P, (2 * k + n + 1) * P)
                            d = bank[:, n * S:(n + 1) * S]
                            pe.matmul(d, up_[0][:, 0, f], band_hi[:, g, 0:S], start=True, stop=False)
                            pe.matmul(d, up_[1][:, 0, f], band_hi[:, g, 0:S], start=False, stop=False)
                            pe.matmul(d[:, 0:16], up_[0][:, 0, f], band_lo[:, g, :], start=False, stop=False)
                            pe.matmul(d[:, P:S], up_[0][:, 1, f], band_hi[:, g, S:S + P], start=False, stop=False)
                            ins = pe.matmul(d[:, P:S], up_[1][:, 1, f], band_hi[:, g, S:S + P], start=False,
                                            stop=True)
                        ins.then_inc(t_ready, 1)

                m, b = m + 8, b + 1
                square_halves(l, m, b, xa, 0, 2)
                diffs(0)
                square_halves(l, m, b, xa, 2, 8)
                m, b = 2 * CH["uq"], BL["qrope"]
                jobs_split(l, JB["cq"] + 1)
                free_acc(l, b)
                for i in range(2):
                    hi, lo = halves(l, m + i)
                    for k in range(2):
                        cols = slice(k * BLK, (k + 1) * BLK)
                        for t in range(TT):
                            tok = slice(t * P, (t + 1) * P)
                            kt = 2 * i + k
                            ins = three(acc[b % 2][:, t, :], xb[0][:, LAT_Q + kt, tok], xb[1][:, LAT_Q + kt, tok],
                                        hi[:, cols], lo[:, cols], kt == 0, kt == LKT - 1)
                    ins.then_inc(w_used, 1)

                def by_feature(m, b, lat_t):
                    parts = []
                    for n in range(2):
                        free_acc(l, b + n)
                        for i in range(2):
                            for k in range(LKT):
                                if n == 0 and i == 0:
                                    parts.append(halves(l, m + k))
                                hi, lo = parts[k]
                                for bank in range(2):
                                    dst = acc[(b + n) % 2][:, bank, i * S:(i + 1) * S]
                                    hd = 4 * n + 2 * bank + i
                                    cols = slice(hd * NOPE, (hd + 1) * NOPE)
                                    ins = three(dst, hi[:, cols], lo[:, cols], xb[0][:, lat_t + k, :],
                                                xb[1][:, lat_t + k, :], k == 0, k == LKT - 1)
                                if n == 1 and i == 1:
                                    ins.then_inc(w_used, 1)
                        if n == 0:
                            ins.then_inc(pair_ready, 1)

                m += 2
                by_feature(m, BL["qnope"], LAT_Q)
                diffs(1)
                jobs_split(l, JB["ckv"] + 1)
                m += LKT
                by_feature(m, BL["knope"], LAT_KV)
                pe.wait_ge(qr_step, 3 * TT * l + 3 * TT)
                for i in range(2):
                    turn(l, JB["qrope"] + i, lambda t, n: qr_tok[:, t, (2 * i + n) * P:(2 * i + n + 1) * P])
                m, b = m + LKT, BL["v"]
                parts = []
                for n in range(2):
                    free_acc(l, b + n)
                    for k in range(LKT):
                        if n == 0:
                            parts.append(halves(l, m + k))
                        hi, lo = parts[k]
                        cols = slice(n * BLK, (n + 1) * BLK)
                        for t in range(TT):
                            tok = slice(t * P, (t + 1) * P)
                            ins = three(acc[(b + n) % 2][:, t, :], xb[0][:, LAT_KV + k, tok],
                                        xb[1][:, LAT_KV + k, tok], hi[:, cols], lo[:, cols], k == 0, k == LKT - 1)
                        if n == 1:
                            ins.then_inc(w_used, 1)
                    if n == 0:
                        ins.then_inc(pair_ready, 1)

                def scores(i):
                    bank = new_job(l, JS[i]) if i > 0 else tps[:, JS[0] % T_BANKS]
                    for t in range(TT):
                        tok = slice(t * P, (t + 1) * P)
                        nk = (t + 1) * P
                        dst = bank[:, t * P:t * P + nk]
                        three(dst, xa[0][:, Q_T + i, tok], xa[1][:, Q_T + i, tok], xa[0][:, K_T + i, 0:nk],
                              xa[1][:, K_T + i, 0:nk], True, False)
                        ins = three(dst, qrt[0][:, i // 2, tok], qrt[1][:, i // 2, tok], krt[0][:, i % 2, 0:nk],
                                    krt[1][:, i % 2, 0:nk], False, True)
                    ins.then_inc(t_ready, 1)

                def outputs(i):
                    assert JT[i] >= JY[i] - T_BANKS
                    jobs_split(l, JT[i])
                    bank = tps[:, JY[i] % T_BANKS]
                    f = slice(i * VDIM, (i + 1) * VDIM)
                    three(bank[:, 0:S], v[0][:, 0, f], v[1][:, 0, f], pt[0][:, 0:S], pt[1][:, 0:S], True, False)
                    three(bank[:, P:S], v[0][:, 1, f], v[1][:, 1, f], pt[0][:, S:3 * P], pt[1][:, S:3 * P],
                          False, True).then_inc(t_ready, 1)

                def probs(i):
                    pe.wait_ge(p_norm, HEADS * l + i + 1)
                    bank = new_job(l, JT[i])
                    for n in range(3):
                        ins = pe.transpose(bank[:, n * P:(n + 1) * P], prob[:, i % 2, n * P:(n + 1) * P],
                                           ident[:, :])
                    ins.then_inc(t_ready, 1)

                def pool_out(i):
                    b = BL["poolw"] + i
                    hi, lo = halves(l, 2 * (CH["poolw"] + i))
                    free_acc(l, b)
                    for g in range(2):
                        for n in range(2):
                            dst = acc[b % 2][:, g, n * S:(n + 1) * S]
                            for k in range(2):
                                cols = slice((2 * g + k) * S + n * P, (2 * g + k) * S + (n + 1) * P)
                                d = DIFF + 4 * i + 2 * g + k
                                ins = three(dst, hi[:, cols], lo[:, cols], xb[0][:, d, :], xb[1][:, d, :], k == 0,
                                            k == 1)
                    ins.then_inc(w_used, 2)

                jobs_split(l, JB["qrope"] + 1)
                block_split(l, BL["v"])
                m_out, b_out = 2 * CH["out"], BL["out"]
                for i in range(HEADS + 2):
                    if i < HEADS:
                        scores(i)
                    if 2 <= i <= HEADS:
                        outputs(i - 2)
                    if 1 <= i <= HEADS:
                        probs(i - 1)
                    if i < 2:
                        pool_out(i)
                    else:
                        j, k = (i - 2) // 4, (i - 2) % 4
                        if j == 0 and k in (0, 2):
                            block_split(l, BL["poolw"] + k // 2)
                        square_half(l, m_out + i - 2, b_out + j, xb, 2 * k, k == 0, False)
                outputs(HEADS - 1)
                m_out += HEADS
                for j in range(2):
                    for k in range(4):
                        if j == 0 and k in (0, 3):
                            jobs_split(l, JY[HEADS - 3 if k == 0 else HEADS - 1])
                        square_half(l, m_out, b_out + j, xb, 8 + 2 * k, False, k == 3)
                        m_out += 1
                        if j == 1 and k == 1:
                            pe.wait_ge(h_ready, 3 * N_BLK * l + N_BLK + 1)
                            turn_h(l, JB["ffn_norm"], 0)
                            turn_h(l, JB["ffn_norm"], 1)
                square_halves(l, m_out, b_out + 2, xb, 0, 2)
                pe.wait_ge(h_ready, 3 * N_BLK * l + N_BLK + 2)
                turn_h(l, JB["ffn_norm"], 2)
                turn_h(l, JB["ffn_norm"], 3)
                square_halves(l, m_out, b_out + 2, xb, 2, 8)
                m_out += 8
                square_halves(l, m_out, b_out + 3, xb, 0, 2)
                pe.wait_ge(h_ready, 3 * N_BLK * l + N_BLK + 3)
                turn_h(l, JB["ffn_norm"], 4)
                turn_h(l, JB["ffn_norm"], 5)
                square_halves(l, m_out, b_out + 3, xb, 2, 8)

                def down(m, b, j, v=None, wait_g=None):
                    for i in range(2):
                        hi, lo = halves(l, m + i, v)
                        if i == 0:
                            free_acc(l, b, v)
                        for k in range(2):
                            cols = slice(k * BLK, (k + 1) * BLK)
                            for t in range(TT):
                                tok = slice(t * P, (t + 1) * P)
                                ft = 2 * i + k
                                ins = three(acc[b % 2][:, t, :], gt[0][:, ft, tok], gt[1][:, ft, tok], hi[:, cols],
                                            lo[:, cols], ft == 0, ft == 3)
                        ins.then_inc(w_used, 1)
                        yield i

                def unit(u, v, with_down):
                    m0 = 2 * CH["ffn"] + (16 if with_down else 0)
                    b0 = BL["ffn"] + (2 if with_down else 0)
                    j0 = JB["ffn"] + (4 if with_down else 0)

                    def turn_rows(rows, b, k):
                        block_split(l, b, v)
                        for i in range(2):
                            turn(l, j0 + k + i, lambda t, n: rows[:, t, (2 * i + n) * P:(2 * i + n + 1) * P], v)

                    if with_down:
                        square_halves(l, m0, b0, xa, 0, 8, v)
                    else:
                        square_halves(l, m0, b0, xa, 0, 2, v)
                        pe.wait_ge(h_ready, 3 * N_BLK * l + N_BLK + 4)
                        turn_h(l, JB["ffn_norm"], 6)
                        turn_h(l, JB["ffn_norm"], 7)
                        square_halves(l, m0, b0, xa, 2, 6, v)
                        jobs_split(l, JB["ffn_norm"] + 7)
                        square_halves(l, m0, b0, xa, 6, 8, v)
                    square_halves(l, m0 + 8, b0 + 1, xa, 0, 3, v)
                    turn_rows(gate_tok, b0, 0)
                    square_halves(l, m0 + 8, b0 + 1, xa, 3, 8, v)
                    if with_down:
                        pe.wait_ge(g_lo, UNITS * l + u)
                        for j in range(N_BLK):
                            for i in down(m0 + 16 + 2 * j, b0 + 2 + j, j, v):
                                if j == 1 and i == 0:
                                    turn_rows(up_tok, b0 + 1, 2)
                    else:
                        turn_rows(up_tok, b0 + 1, 2)

                jobs_split(l, JB["ffn_norm"] + 5)
                unit(0, 0, False)
                with pe.Fori(1, UNITS) as u:
                    unit(u, u - 1, True)
                m, b = 2 * (CH["ple"] - N_BLK), BL["ple"] - N_BLK
                pe.wait_ge(g_lo, UNITS * l + UNITS)
                for j in range(N_BLK):
                    for i in down(m + 2 * j, b + j, j):
                        if i == 0 and j == 0:
                            pe.wait_ge(p_landed, 16 * l + 16)
                            turn(l, JB["p"], lambda t, n: p_tok[:, t, n * P:(n + 1) * P])
                        elif i == 0:
                            pe.wait_ge(h_ready, 3 * N_BLK * l + N_BLK + N_BLK + j)
                            turn_h(l, JB["ple_norm"], 2 * j - 2)
                            turn_h(l, JB["ple_norm"], 2 * j - 1)

                m, b = 2 * CH["ple"], BL["ple"]
                jobs_split(l, JB["p"])
                for i in range(2):
                    parts = [halves(l, m), None]
                    for n in range(2):
                        free_acc(l, b + n)
                        cols = slice(n * BLK, (n + 1) * BLK)
                        for k in range(2):
                            if n == 0 and k == 1:
                                parts[1] = halves(l, m + 1)
                            hi, lo = parts[k]
                            for t in range(TT):
                                tok = slice(t * P, (t + 1) * P)
                                ins = three(acc[(b + n) % 2][:, t, :], ppt[0][:, k, tok], ppt[1][:, k, tok],
                                            hi[:, cols], lo[:, cols], k == 0, k == 1)
                            if n == 1:
                                ins.then_inc(w_used, 1)
                        if n == 0:
                            ins.then_inc(pair_ready, 1)
                    m, b = m + 2, b + 2
                    if i == 0:
                        pe.wait_ge(h_ready, 3 * N_BLK * l + N_BLK + 2 * N_BLK)
                        turn_h(l, JB["ple_norm"], 6)
                        turn_h(l, JB["ple_norm"], 7)
                        jobs_split(l, JB["ple_norm"] + 5)
                    for j in range(2):
                        square_halves(l, m, b, xb, 0, 6)
                        if i == 0 and j == 0:
                            jobs_split(l, JB["ple_norm"] + 7)
                        square_halves(l, m, b, xb, 6, 8)
                        m, b = m + 8, b + 1


_INS = ['x', 'p', 'positions', 'norm_mix_g', 'w_in', 'pool_w', 'pool_scale', 'q_norm_g', 'w_uq', 'kv_norm_g',
        'w_ukv', 'w_out', 'norm_ffn_g', 'w_up', 'conv_w', 'conv_b', 'w_down', 'norm_ple_g', 'w_ple',
        'w_ple_gate', 'final_norm_g']


def kernel(**inputs):
    import concourse.bacc as _bacc
    from concourse.bass_utils import run_bass_kernel_spmd as _run

    nc = _bacc.Bacc("TRN2", target_bir_lowering=False, num_devices=1)
    arrays, args = {}, []
    for name in _INS:
        a = np.ascontiguousarray(inputs[name])
        arrays[f"in_{name}"] = a
        args.append(nc.dram_tensor(f"in_{name}", a.shape, mybir.dt.from_np(a.dtype), kind="ExternalInput").ap())
    out = nc.dram_tensor("out_0", arrays["in_x"].shape, F32, kind="ExternalOutput").ap()
    build(nc, *args, out)
    r = _run(nc, [arrays], core_ids=[0])
    return r.results[0]["out_0"]
```

```python
from contextlib import ExitStack

import numpy as np

import concourse.bass as bass
from concourse import mybir

P = 128
F32 = mybir.dt.float32
F32R = mybir.dt.float32r
I32 = mybir.dt.int32
ACT = mybir.ActivationFunctionType
ALU = mybir.AluOpType

POOL_WINDOWS = (2, 4, 8, 16)
HEADS, NOPE, ROPE, VDIM = 8, 128, 64, 128
THETA = 10000.0
EPS = 1e-6
MASKED = -3.0e38

CHUNK = 2048
HALF = CHUNK // 2
RAW_SLOTS = 4
HALF_SLOTS = 6
AHEAD = 4
POOL_SETUP = 44 + 4 * len(POOL_WINDOWS) + 4 * len(POOL_WINDOWS)
DVE_REDUCED = 18
BLK = 512
T_BANKS = 4


def layer_plan(d_model, d_ff):
    n_blk = d_model // BLK
    units = d_ff // BLK
    kt = d_model // P
    per_block = kt // 4
    c, chunk = 0, {}
    for name, n in (("cq", per_block), ("ckv", per_block), ("kr", 1), ("pool", 2 * per_block), ("uq", 3),
                    ("ukv", 4), ("poolw", 2), ("out", n_blk * per_block), ("ffn", units * 3 * per_block),
                    ("ple", n_blk * per_block + 2)):
        chunk[name] = c
        c += n
    b, block = 0, {}
    for name, n in (("cq", 1), ("ckv", 1), ("kr", 1), ("pool", 2), ("qrope", 1), ("qnope", 2), ("knope", 2),
                    ("v", 2), ("poolw", 2), ("out", n_blk), ("ffn", units * (2 + n_blk)), ("ple", 2 * n_blk)):
        block[name] = b
        b += n
    j, job = 0, {}
    for name, n in (("mix", kt // 2), ("cq", 2), ("kr", 1), ("ckv", 2), ("diff", 4), ("qrope", 2),
                    ("heads", 3 * HEADS), ("ffn_norm", kt // 2), ("ffn", 4 * units), ("p", 1), ("ple_norm", kt // 2)):
        job[name] = j
        j += n
    last = {}
    for name, n in (("cq", 1), ("ckv", 1), ("pool", 2)):
        for i in range(n):
            last[block[name] + i] = 2 * (chunk[name] + (i + 1) * per_block) - 1
    last[block["kr"]] = 2 * chunk["kr"]
    last[block["qrope"]] = 2 * chunk["uq"] + 1
    last[block["qnope"] + 1] = 2 * chunk["uq"] + 5
    last[block["knope"] + 1] = 2 * chunk["ukv"] + 3
    last[block["v"] + 1] = 2 * chunk["ukv"] + 7
    for i in range(2):
        last[block["poolw"] + i] = 2 * (chunk["poolw"] + i)
    for name, ends in (("out", (11, 15, 23, 31)), ("ffn", (7, 15, 23, 31, 33, 35, 37, 39)),
                       ("ple", (1, 1, 9, 17, 19, 19, 27, 35))):
        for i, m in enumerate(ends):
            last[block[name] + i] = 2 * chunk[name] + m
    for i in range(n_blk):
        last[block["ple"] - n_blk + i] = 2 * (chunk["ple"] - n_blk + i) + 1
    return dict(last=last, n_blk=n_blk, units=units, kt=kt, chunk=chunk, chunks=c, block=block, blocks=b, job=job, jobs=j)


def head_jobs(first):
    s, t, y, n = {}, {}, {}, first
    for i in range(HEADS + 2):
        if i < HEADS:
            s[i] = n
            n += 1
        if i >= 2:
            y[i - 2] = n
            n += 1
        if 1 <= i <= HEADS:
            t[i - 1] = n
            n += 1
    return s, t, y


def build(nc, x, p, positions, norm_mix_g, w_in, pool_w, pool_scale, q_norm_g, w_uq, kv_norm_g, w_ukv,
          w_out, norm_ffn_g, w_up, conv_w, conv_b, w_down, norm_ple_g, w_ple, w_ple_gate, final_norm_g, out):
    L, D, _ = w_in.shape
    S = x.shape[1]
    D_FF = w_down.shape[1]
    D_POOL = pool_scale.shape[1]
    LORA = w_uq.shape[1]
    PLE = w_ple.shape[1]
    TT = S // P
    plan = layer_plan(D, D_FF)
    N_BLK, UNITS, KT = plan["n_blk"], plan["units"], plan["kt"]
    CH, BL, JB = plan["chunk"], plan["block"], plan["job"]
    CHUNKS, BLOCKS, JOBS = plan["chunks"], plan["blocks"], plan["jobs"]
    LKT = LORA // P
    PKT = D_POOL // P
    UNIT_CHUNKS = 3 * (KT // 4)
    UNIT_HALVES = 2 * UNIT_CHUNKS
    SCALE = float(NOPE + ROPE) ** -0.5
    assert TT == 2 and LORA == BLK and D_POOL == 2 * BLK and PLE == 2 * P and LKT == 4
    assert CHUNKS % RAW_SLOTS == 0 and 2 * CHUNKS % HALF_SLOTS == 0 and UNIT_CHUNKS % RAW_SLOTS == 0
    assert BLOCKS % 2 == 0 and JOBS % T_BANKS == 0
    JS, JT, JY = head_jobs(JB["heads"])
    LAST = plan["last"]

    G_MIX, G_FFN, G_PLE = 0, KT, 2 * KT
    POOL_S = 3 * KT
    FKT = D_FF // P
    TAP = [POOL_S + PKT + t * FKT for t in range(3)]
    BIAS = TAP[2] + FKT
    G_Q = BIAS + FKT
    G_KV = G_Q + LKT
    N_PRM = G_KV + LKT
    ROWS_G = 3 * KT + PKT

    with ExitStack() as ctx:
        def sb(name, shape, dt=F32, scope=ctx):
            return scope.enter_context(nc.sbuf_tensor(name, shape, dt))

        def sem(name):
            return ctx.enter_context(nc.semaphore(name))

        raw = sb("raw", [P, RAW_SLOTS, CHUNK])
        w_hi = sb("w_hi", [P, HALF_SLOTS, HALF], F32R)
        w_lo = sb("w_lo", [P, HALF_SLOTS, HALF], F32R)
        xa = (sb("xa_hi", [P, KT, S], F32R), sb("xa_lo", [P, KT, S], F32R))
        xb = (sb("xb_hi", [P, KT, S], F32R), sb("xb_lo", [P, KT, S], F32R))
        h = sb("h", [P, TT, D])
        ident = sb("ident", [P, P])
        mask = sb("mask", [P, 2 * P])
        band_hi = sb("band_hi", [P, len(POOL_WINDOWS), 3 * P], F32R)
        band_lo = sb("band_lo", [P, len(POOL_WINDOWS), 16], F32R)
        cos = sb("cos", [P, TT, ROPE // 2])
        sin = sb("sin", [P, TT, ROPE // 2])
        prm_all = sb("prm_all", [P, L + 1, N_PRM])
        prm = prm_all[:, L, :]
        krt = (sb("krt_hi", [P, 2, S], F32R), sb("krt_lo", [P, 2, S], F32R))
        sumsq = sb("sumsq", [P, TT, N_BLK])
        sumsq_lat = sb("sumsq_lat", [P, 2, TT])
        rstd = {n: sb(f"rstd_{n}", [P, TT]) for n in ("mix", "q", "kv", "ffn", "ple", "final")}
        part = sb("part", [P, TT, 2])
        mean = sb("mean", [P, TT])
        consts = sb("consts", [P, 5, TT])
        C_D, C_LORA, C_EPS, C_POWER, C_HALF = range(5)
        mx = sb("mx", [P, 2, TT])
        nmx = sb("nmx", [P, 2, TT])
        psums = sb("psums", [P, 2, TT])
        prec = sb("prec", [P, 2, TT])

        with ExitStack() as scope:
            rows_g = sb("rows_g", [ROWS_G, L, P], scope=scope)
            rows_c = [sb(f"rows_c{i}", [2 * FKT, L, P], scope=scope) for i in range(2)]
            band = sb("band", [P, len(POOL_WINDOWS), 3 * P], scope=scope)
            inv_cnt = sb("inv_cnt", [P, 16], scope=scope)
            pos_i = sb("pos_i", [P, TT], I32, scope=scope)
            pos_f = sb("pos_f", [P, TT], scope=scope)
            inv_freq = sb("inv_freq", [P, ROPE // 2], scope=scope)
            ang = sb("ang", [P, TT, ROPE // 2], scope=scope)
            turns = sb("turns", [P, 2, TT, ROPE // 2], scope=scope)
            red = sb("red", [P, 2, TT, ROPE // 2], scope=scope)
            table_word = sb("table_word", [P, 1], scope=scope)
            sq_x = sb("sq_x", [P, TT, N_BLK - 1, BLK], scope=scope)
        with ExitStack() as scope:
            with ExitStack() as early:
                lat = sb("lat", [P, 2, TT, BLK], scope=early)
                kr_tok = sb("kr_tok", [P, TT, P], scope=early)
                kr_in = sb("kr_in", [P, TT, ROPE], scope=early)
                kr_tmp = sb("kr_tmp", [P, 2, TT, ROPE // 2], scope=early)
                sq_lat = sb("sq_lat", [P, TT, BLK], scope=early)
            with ExitStack() as early:
                qr_tok = sb("qr_tok", [P, TT, BLK], scope=early)
                qr_tmp = sb("qr_tmp", [P, 2, BLK // 2], scope=early)
            v = (sb("v_hi", [P, TT, HEADS * VDIM], F32R, scope=scope),
                 sb("v_lo", [P, TT, HEADS * VDIM], F32R, scope=scope))
            qrt = (sb("qrt_hi", [P, HEADS // 2, S], F32R, scope=scope),
                   sb("qrt_lo", [P, HEADS // 2, S], F32R, scope=scope))
            with ExitStack() as early:
                up_ = (sb("upool_hi", [P, TT, BLK], F32R, scope=early),
                       sb("upool_lo", [P, TT, BLK], F32R, scope=early))
            prob = sb("prob", [P, 2, 3 * P], scope=scope)
            pt = (sb("pt_hi", [P, 3 * P], F32R, scope=scope), sb("pt_lo", [P, 3 * P], F32R, scope=scope))
        with ExitStack() as scope:
            gate_tok = sb("gate_tok", [P, TT, BLK], scope=scope)
            up_tok = sb("up_tok", [P, TT, BLK], scope=scope)
            conv = sb("conv", [P, 4, S], scope=scope)
            sig = sb("sig", [P, 4, S], scope=scope)
            gt = (sb("gt_hi", [P, 4, S], F32R, scope=scope), sb("gt_lo", [P, 4, S], F32R, scope=scope))
            p_tok = sb("p_tok", [P, TT, PLE], scope=scope)
            ppt = (sb("ppt_hi", [P, 2, S], F32R, scope=scope), sb("ppt_lo", [P, 2, S], F32R, scope=scope))
            sq_h = sb("sq_h", [P, TT, BLK], mybir.dt.bfloat16, scope=scope)
        with ExitStack() as scope:
            pw = sb("pw", [P, 2, TT, 2 * BLK], scope=scope)
            sg = sb("sg", [P, 2, TT, BLK], scope=scope)
        with ExitStack() as scope:
            fin_g = sb("fin_g", [P, D], scope=scope)

        acc = [ctx.enter_context(nc.psum_tensor(f"acc{i}", [P, 2, BLK], F32)) for i in range(2)]
        tps = ctx.enter_context(nc.psum_tensor("tps", [P, T_BANKS, BLK], F32))

        raw_landed = [sem(f"raw_landed{i}") for i in range(RAW_SLOTS)]
        slot_seen = sem("slot_seen")
        scores_seen = sem("scores_seen")
        hi_done = sem("hi_done")
        lo_done = sem("lo_done")
        w_used = sem("w_used")
        pair_ready = sem("pair_ready")
        acc_free = [sem(f"acc_free{i}") for i in range(2)]
        t_ready = sem("t_ready")
        t_done = sem("t_done")
        x_landed = [sem(f"x_landed{i}") for i in range(N_BLK)]
        rows_landed = sem("rows_landed")
        conv_landed = sem("conv_landed")
        lat_landed = sem("lat_landed")
        pos_landed = sem("pos_landed")
        p_landed = sem("p_landed")
        fin_landed = sem("fin_landed")
        stored = sem("stored")
        pool_setup = sem("pool_setup")
        dve_setup = sem("dve_setup")
        act_setup = sem("act_setup")
        prm_t = sem("prm_t")
        prm_ready = sem("prm_ready")
        h_ready = sem("h_ready")
        x_sq = sem("x_sq")
        sq_done = sem("sq_done")
        sq_lat_done = sem("sq_lat_done")
        rstd_step = sem("rstd_step")
        rstd_done = sem("rstd_done")
        lat_norm = sem("lat_norm")
        hT_hi = sem("hT_hi")
        lat_hi = sem("lat_hi")
        kr_step = sem("kr_step")
        kr_hi = sem("kr_hi")
        upool_hi = sem("upool_hi")
        diff_hi = sem("diff_hi")
        qr_step = sem("qr_step")
        qr_hi = sem("qr_hi")
        qk_hi = sem("qk_hi")
        v_hi = sem("v_hi")
        ypool_hi = sem("ypool_hi")
        s_ready = sem("s_ready")
        e_done = sem("e_done")
        p_rec = sem("p_rec")
        p_norm = sem("p_norm")
        pt_hi = sem("pt_hi")
        y_hi = sem("y_hi")
        conv_step = sem("conv_step")
        silu_done = sem("silu_done")
        conv_done = sem("conv_done")
        tanh_done = sem("tanh_done")
        g_done = sem("g_done")
        g_hi = sem("g_hi")
        g_lo = sem("g_lo")
        p_hi = sem("p_hi")
        ple_step = sem("ple_step")
        fin_done = sem("fin_done")

        LAT_Q, LAT_KV = 0, LKT
        DIFF = 2 * LKT
        Q_T, K_T = 0, HEADS
        HJ = KT // 2

        def half_of(m):
            return m % HALF_SLOTS

        def block_ready(eng, l, b, v=None):
            base = l * (2 * CHUNKS) if v is None else l * (2 * CHUNKS) + v * UNIT_HALVES
            eng.wait_ge(w_used, base + (HALF_SLOTS + LAST[b] + 1))

        def scalar_of(col):
            return prm[:, col:col + 1]

        def load_x(eng, j):
            cols = slice(j * BLK, (j + 1) * BLK)
            eng.dma_start(h[:, :, cols], x.rearrange("o (t p) n -> p (o t) n", p=P)[:, :, cols]).then_inc(
                x_landed[j], 16)

        block = ctx.enter_context(nc.Block())

        @block.sync
        def _(sp):
            def load(l, c, pieces):
                slot = c % RAW_SLOTS
                sp.wait_ge(lo_done, 2 * CHUNKS * l + 2 * c + 2)
                sp.sem_inc(slot_seen, 1)
                src, width, shape = pieces
                dst = raw[:, slot, 0:width]
                if shape is not None:
                    dst = dst.rearrange("p (a b) -> p a b", b=shape)
                sp.dma_start(dst, src).then_inc(raw_landed[slot], 16)

            def rows(w, l, k0, nk, cols, n):
                view = w.rearrange("l (k p) n -> l p k n", p=P)
                return view[bass.ds(l, 1), :, bass.ds(k0, nk), bass.ds(cols, n)].rearrange("l p k n -> p (l k) n")

            def square(w, l, k4, col):
                return rows(w, l, 4 * k4, 4, col, BLK), CHUNK, BLK

            def heads_cols(w, l, width, k0, nk, c0, n):
                view = w.rearrange("l (p k) (h c) -> l p (k h) c", k=LKT, c=width)
                return view[bass.ds(l, 1), :, HEADS * k0:HEADS * (k0 + nk), c0:c0 + n].rearrange(
                    "l p k n -> p (l k) n")

            for i, g in enumerate((norm_mix_g, norm_ffn_g, norm_ple_g)):
                sp.dma_start(rows_g[KT * i:KT * (i + 1)], g.rearrange("l (k p) -> k l p", p=P)).then_inc(
                    rows_landed, 16)
            sp.dma_start(rows_g[POOL_S:POOL_S + PKT], pool_scale.rearrange("l (k p) -> k l p", p=P)).then_inc(
                rows_landed, 16)

            sp.dma_start(rows_c[0][:, :, :], conv_w[:, 0:2].rearrange("l t (k p) -> (t k) l p", p=P)).then_inc(
                conv_landed, 16)
            sp.dma_start(rows_c[1][0:FKT], conv_w[:, 2].rearrange("l (k p) -> k l p", p=P)).then_inc(conv_landed, 16)
            sp.dma_start(rows_c[1][FKT:2 * FKT], conv_b.rearrange("l (k p) -> k l p", p=P)).then_inc(
                conv_landed, 16)

            with sp.Fori(0, L) as l:
                c = CH["cq"]
                for col in (D_POOL, D_POOL + LORA):
                    for k in range(KT // 4):
                        load(l, c, square(w_in, l, k, col))
                        c += 1
                load(l, c, (rows(w_in, l, 0, KT, D_POOL + 2 * LORA, ROPE), KT * ROPE, ROPE))
                c += 1
                for col in (0, BLK):
                    for k in range(KT // 4):
                        load(l, c, square(w_in, l, k, col))
                        c += 1
                load(l, c, (heads_cols(w_uq, l, NOPE + ROPE, 0, LKT, NOPE, ROPE), CHUNK, ROPE))
                for i in range(2):
                    load(l, c + 1 + i, (heads_cols(w_uq, l, NOPE + ROPE, 2 * i, 2, 0, NOPE), CHUNK, NOPE))
                c += 3
                for c0 in (0, NOPE):
                    for i in range(2):
                        load(l, c, (heads_cols(w_ukv, l, NOPE + VDIM, 2 * i, 2, c0, NOPE), CHUNK, NOPE))
                        c += 1
                for i in range(2):
                    src = pool_w[bass.ds(l, 1), 2 * i:2 * i + 2].rearrange("l g (k p) n -> p (l g k) n", p=P)
                    load(l, c, (src, HALF, 2 * P))
                    c += 1
                for j, k in ([(j, k) for k0 in (0, 2) for j in (0, 1) for k in (k0, k0 + 1)]
                             + [(j, k) for j in (2, 3) for k in range(4)]):
                    load(l, c, square(w_out, l, k, j * BLK))
                    c += 1

                def gate_up(l, u, c):
                    for col in (0, D_FF):
                        for k in range(KT // 4):
                            load(l, c, (rows(w_up, l, 4 * k, 4, col + u * BLK, BLK), CHUNK, BLK))
                            c += 1
                    return c

                def load_at(l, c, before, pieces):
                    slot = c % RAW_SLOTS
                    sp.wait_ge(lo_done, 2 * CHUNKS * l + 2 * before + 2 * c + 2)
                    sp.sem_inc(slot_seen, 1)
                    src, width, shape = pieces
                    sp.dma_start(raw[:, slot, 0:width].rearrange("p (a b) -> p a b", b=shape),
                                 src).then_inc(raw_landed[slot], 16)

                c = gate_up(l, 0, c)
                with sp.Fori(1, UNITS) as u:
                    before = (u - 1) * UNIT_CHUNKS
                    n = c
                    for col in (0, D_FF):
                        for k in range(KT // 4):
                            load_at(l, n, before, (rows(w_up, l, 4 * k, 4, col + u * BLK, BLK), CHUNK, BLK))
                            n += 1
                    for j in range(N_BLK):
                        load_at(l, n, before, (rows(w_down, l, (u - 1) * 4, 4, j * BLK, BLK), CHUNK, BLK))
                        n += 1
                c += UNIT_CHUNKS * (UNITS - 1)
                for j in range(N_BLK):
                    load(l, c, (rows(w_down, l, 4 * (UNITS - 1), 4, j * BLK, BLK), CHUNK, BLK))
                    c += 1
                for i in range(2):
                    load(l, c, (rows(w_ple, l, 0, 2, i * 2 * BLK, 2 * BLK), CHUNK, 2 * BLK))
                    c += 1
                    for j in (2 * i, 2 * i + 1):
                        for k in range(KT // 4):
                            load(l, c, square(w_ple_gate, l, k, j * BLK))
                            c += 1
                assert c == CHUNKS
            for c in range(AHEAD // 2):
                sp.wait_ge(lo_done, 2 * CHUNKS * L + 2 * c + 2)
                sp.sem_inc(raw_landed[c % RAW_SLOTS], 16)
            o_v = out.rearrange("o (t p) n -> p (o t) n", p=P)
            for j in range(N_BLK):
                sp.wait_ge(fin_done, TT * (j + 1))
                sp.dma_start(o_v[:, :, j * BLK:(j + 1) * BLK], h[:, :, j * BLK:(j + 1) * BLK]).then_inc(stored, 16)
            sp.wait_ge(stored, 16 * N_BLK)

        @block.gpsimd
        def _(pool):
            n = [0]
            def step(ins):
                n[0] += 1
                ins.then_inc(pool_setup, 1)

            def after():
                pool.wait_ge(pool_setup, n[0])

            step(pool.memset(ident[:, :], 0.0))
            step(pool.memset(mask[:, :], 0.0))
            for i, value in enumerate((1.0 / D, 1.0 / LORA, EPS, -0.5, 0.5)):
                step(pool.memset(consts[:, i, :], value))
            step(pool.iota(inv_cnt[:, :], [[1, 16]], base=1, channel_multiplier=0,
                           allow_small_or_imprecise_dtypes=True))
            after()
            step(pool.affine_select(out=ident[:, :], in_=ident[:, :], compare_op=ALU.not_equal, fill=1.0,
                                    base=0, pattern=[[-1, P]], channel_multiplier=1))
            step(pool.affine_select(out=mask[:, P:2 * P], in_=mask[:, P:2 * P], compare_op=ALU.is_ge,
                                    fill=MASKED, base=0, pattern=[[-1, P]], channel_multiplier=1))
            for i in range(ROPE // 2):
                f = np.float32(1.0) / np.power(np.float32(THETA), np.float32(2 * i) / np.float32(ROPE))
                step(pool.memset(inv_freq[:, i:i + 1], float(f)))
            for j in range(2, N_BLK):
                load_x(pool, j)
            for c0, g in ((G_Q, q_norm_g), (G_KV, kv_norm_g)):
                pool.dma_start(prm_all[:, 0:L, c0:c0 + LKT], g.rearrange("l (p k) -> p l k", k=LKT)).then_inc(
                    lat_landed, 16)
            for g, w in enumerate(POOL_WINDOWS):
                step(pool.memset(band[:, g, :], 1.0 / w))
            after()
            pool.wait_ge(dve_setup, 1)
            for g, w in enumerate(POOL_WINDOWS):
                step(pool.tensor_copy(band[:, g, 0:w], inv_cnt[:, 0:w]))
            after()
            for g, w in enumerate(POOL_WINDOWS):
                for c0, cn in ((0, 2 * P), (2 * P, P)):
                    b = band[:, g, c0:c0 + cn]
                    step(pool.affine_select(out=b, in_=b, compare_op=ALU.is_ge, fill=0.0, base=0,
                                            pattern=[[1, cn]], channel_multiplier=-1))
                    after()
                    step(pool.affine_select(out=b, in_=b, compare_op=ALU.is_ge, fill=0.0, base=w - 1,
                                            pattern=[[-1, cn]], channel_multiplier=1))
            after()
            for g in range(len(POOL_WINDOWS)):
                for c0 in (0, 2 * P):
                    step(pool.tensor_tensor(band[:, g, c0:c0 + P], band[:, g, c0:c0 + P], ident[:, :],
                                            ALU.subtract))
            after()
            step(pool.tensor_copy(band_hi[:, :, :], band[:, :, :]))
            after()
            step(pool.tensor_tensor(band_lo[:, :, :], band[:, :, 0:16], band_hi[:, :, 0:16].bitcast(F32),
                                    ALU.subtract))
            assert n[0] == POOL_SETUP
            for j in range(N_BLK - 1):
                pool.wait_ge(x_landed[j], 16)
                hb = h[:, :, j * BLK:(j + 1) * BLK]
                pool.tensor_tensor(sq_x[:, :, j, :], hb, hb, ALU.mult).then_inc(x_sq, 1)
            steps, width = N_BLK - 1, BLK // 2
            while width:
                pool.wait_ge(x_sq, steps)
                dst = sq_x[:, :, :, 0:width] if width > 1 else sumsq[:, :, 0:N_BLK - 1].unsqueeze(3)
                pool.tensor_tensor(dst, sq_x[:, :, :, 0:width], sq_x[:, :, :, width:2 * width],
                                   ALU.add).then_inc(x_sq, 1)
                steps, width = steps + 1, width // 2
            pool.wait_ge(x_sq, steps)

            def factor(done, src, dst, n_terms, step0, halved=False):
                k = 0
                pool.wait_ge(rstd_done, done + 1)
                if src.shape[-1] == N_BLK and len(src.shape) == 3:
                    pool.tensor_tensor(part[:, :, :], src[:, :, 0:2], src[:, :, 2:4], ALU.add).then_inc(rstd_step, 1)
                    pool.wait_ge(rstd_step, step0 + 1)
                    pool.tensor_tensor(mean[:, :], part[:, :, 0], part[:, :, 1], ALU.add).then_inc(rstd_step, 1)
                    pool.wait_ge(rstd_step, step0 + 2)
                    k, src = 2, mean[:, :]
                pool.tensor_tensor(mean[:, :], src, consts[:, n_terms, :], ALU.mult).then_inc(rstd_step, 1)
                pool.wait_ge(rstd_step, step0 + k + 1)
                pool.tensor_tensor(mean[:, :], mean[:, :], consts[:, C_EPS, :], ALU.add).then_inc(rstd_step, 1)
                pool.wait_ge(rstd_step, step0 + k + 2)
                ins = pool.tensor_tensor(dst[:, :], mean[:, :], consts[:, C_POWER, :], ALU.pow)
                if halved:
                    ins.then_inc(rstd_step, 1)
                    pool.wait_ge(rstd_step, step0 + k + 3)
                    ins = pool.tensor_tensor(dst[:, :], dst[:, :], consts[:, C_HALF, :], ALU.mult)
                ins.then_inc(rstd_done, 1)

            STEPS = 4 + 2 + 2 + 4 + 5
            p_v = p.rearrange("l o (t p) n -> l p (o t) n", p=P)
            pool.sem_inc(rstd_done, 1)
            with pool.Fori(0, L) as l:
                pool.wait_ge(sq_done, TT * (3 * N_BLK * l + 2))
                factor(5 * l + 0, sumsq[:, :, :], rstd["mix"], C_D, STEPS * l)
                pool.wait_ge(sq_lat_done, 2 * TT * l + TT)
                factor(5 * l + 1, sumsq_lat[:, 0, :], rstd["q"], C_LORA, STEPS * l + 4)
                pool.wait_ge(sq_lat_done, 2 * TT * l + 2 * TT)
                factor(5 * l + 2, sumsq_lat[:, 1, :], rstd["kv"], C_LORA, STEPS * l + 6)
                pool.wait_ge(sq_done, TT * (3 * N_BLK * l + N_BLK + 2))
                factor(5 * l + 3, sumsq[:, :, :], rstd["ffn"], C_D, STEPS * l + 8)
                pool.wait_ge(t_ready, JOBS * l + JB["ffn"] + 1)
                pool.dma_start(p_tok[:, :, :], p_v[bass.ds(l, 1)].rearrange("l p t n -> p (l t) n")).then_inc(
                    p_landed, 16)
                pool.wait_ge(g_hi, UNITS * l + UNITS)
                pool.tensor_tensor(xa[1][:, 0:4, :], conv[:, :, :], xa[0][:, 0:4, :].bitcast(F32),
                                   ALU.subtract).then_inc(g_lo, 1)
                pool.wait_ge(sq_done, TT * (3 * N_BLK * l + 2 * N_BLK + 2))
                factor(5 * l + 4, sumsq[:, :, :], rstd["ple"], C_D, STEPS * l + 12, halved=True)
            pool.wait_ge(h_ready, 3 * N_BLK * L + 2)
            pool.dma_start(fin_g[:, :], final_norm_g.rearrange("(o n) -> o n", o=1).broadcast_to([P, D])).then_inc(
                fin_landed, 16)
            pool.wait_ge(rstd_done, 5 * L + 1)
            pool.wait_ge(sq_done, TT * (3 * N_BLK * L + 1))
            k = STEPS * L
            for dst, a, b, op in ((part[:, :, 0], sumsq[:, :, 0], sumsq[:, :, 1], ALU.add),
                                  (part[:, :, 1], part[:, :, 0], sumsq[:, :, 2], ALU.add),
                                  (part[:, :, 0], part[:, :, 1], consts[:, C_D, :], ALU.mult),
                                  (part[:, :, 1], part[:, :, 0], consts[:, C_EPS, :], ALU.add)):
                pool.tensor_tensor(dst, a, b, op).then_inc(rstd_step, 1)
                k += 1
                pool.wait_ge(rstd_step, k)
            pool.wait_ge(sq_done, TT * (3 * N_BLK * L + 2))
            for dst, a, b, op in ((mean[:, :], sumsq[:, :, 3], consts[:, C_D, :], ALU.mult),
                                  (part[:, :, 0], mean[:, :], part[:, :, 1], ALU.add)):
                pool.tensor_tensor(dst, a, b, op).then_inc(rstd_step, 1)
                k += 1
                pool.wait_ge(rstd_step, k)
            pool.tensor_tensor(rstd["final"][:, :], part[:, :, 0], consts[:, C_POWER, :], ALU.pow).then_inc(
                rstd_done, 1)

        @block.scalar
        def _(act):
            copy = nc.scalar.activation

            with nc.allow_non_contiguous_dma(reason="256 positions, once"):
                act.dma_start(pos_i[:, :], positions.rearrange("o (t p) -> p (o t)", p=P)).then_inc(pos_landed, 16)
            load_x(act, 0)
            load_x(act, 1)

            def split(l, m):
                c = m // 2
                act.wait_ge(raw_landed[c % RAW_SLOTS], l * (CHUNKS // RAW_SLOTS * 16) + (c // RAW_SLOTS * 16 + 16))
                act.wait_ge(w_used, l * (2 * CHUNKS) + m + 1)
                copy(w_hi[:, half_of(m), :], raw[:, c % RAW_SLOTS, (m % 2) * HALF:(m % 2 + 1) * HALF],
                     ACT.Copy).then_inc(hi_done, 1)

            def steps(l, a, b):
                for m in range(a, b):
                    split(l, m + AHEAD)

            act.sem_inc(sq_done, TT)
            act.wait_ge(dve_setup, DVE_REDUCED)
            copy(sin[:, :, :], red[:, 0], ACT.Sin).then_inc(act_setup, 1)
            copy(cos[:, :, :], red[:, 1], ACT.Sin).then_inc(act_setup, 1)
            copy(table_word[:, :], inv_freq[:, 0:1], ACT.Tanh)

            def gained(l, job, dst, kt, gain, done):
                act.wait_ge(t_ready, JOBS * l + job + 1)
                for i in range(2):
                    ins = copy(dst[0][:, kt + i, :], tps[:, job % T_BANKS, i * S:(i + 1) * S], ACT.Copy,
                               scale=scalar_of(gain + i))
                ins.then_inc(done, 1)

            def mix_job(l, i):
                gained(l, JB["mix"] + i, xa, 2 * i, G_MIX + 2 * i, hT_hi)

            act.wait_ge(prm_ready, 1)
            mix_job(0, 0)
            mix_job(0, 1)
            split(0, 0)
            split(0, 1)
            mix_job(0, 2)
            mix_job(0, 3)

            def squares(l, j, number):
                act.wait_ge(h_ready, 3 * N_BLK * l + N_BLK + number)
                for t in range(TT):
                    act.wait_ge(sq_done, TT * (3 * N_BLK * l + number) + t + 1)
                    copy(sq_h[:, t, :], h[:, t, j * BLK:(j + 1) * BLK], ACT.Square,
                         accum_out=sumsq[:, t, j:j + 1]).then_inc(sq_done, 1)

            def whole(l, b, bank, dst, done):
                copy(dst, acc[b % 2][:, bank, :], ACT.Copy).then_inc(done, 1)

            with act.Fori(0, L) as l:
                act.wait_ge(prm_ready, l + 2)
                steps(l, -2, 2)
                for i in range(4, 6):
                    mix_job(l, i)
                act.wait_ge(x_landed[N_BLK - 1], 16)
                squares(l, N_BLK - 1, 0)
                steps(l, 2, 4)
                for i in range(6, 8):
                    mix_job(l, i)
                steps(l, 4, 8)

                def latent(i):
                    b = BL["cq"] + i
                    block_ready(act, l, b)
                    if i == 0:
                        act.wait_ge(rstd_done, 5 * l + 2)
                    for t in range(TT):
                        copy(lat[:, i, t, :], acc[b % 2][:, t, :], ACT.Copy,
                             scale=rstd["mix"][:, t:t + 1]).then_inc(acc_free[b % 2], 1)
                    for t in range(TT):
                        act.wait_ge(acc_free[b % 2], BLOCKS * l + 2 * (b // 2 + 1) + t + 1)
                        if i == 1:
                            act.wait_ge(sq_lat_done, 2 * TT * l + t + 1)
                        copy(sq_lat[:, t, :], lat[:, i, t, :], ACT.Square,
                             accum_out=sumsq_lat[:, i, t:t + 1]).then_inc(sq_lat_done, 1)

                latent(0)
                steps(l, 8, 12)
                for i in range(2):
                    gained(l, JB["cq"] + i, xb, LAT_Q + 2 * i, G_Q + 2 * i, lat_hi)
                steps(l, 12, 16)
                latent(1)
                steps(l, 16, 18)
                b = BL["kr"]
                block_ready(act, l, b)
                for t in range(TT):
                    ins = copy(kr_in[:, t, :], acc[b % 2][:, t, 0:ROPE], ACT.Copy,
                               scale=rstd["mix"][:, t:t + 1])
                    ins.then_inc(acc_free[b % 2], 1)
                steps(l, 18, 20)
                act.wait_ge(t_ready, JOBS * l + JB["kr"] + 1)
                bank = tps[:, JB["kr"] % T_BANKS, 0:S]
                copy(krt[0][0:ROPE, 0, :], bank[0:ROPE], ACT.Copy)
                copy(krt[0][ROPE:P, 1, :], bank[ROPE:P], ACT.Copy).then_inc(kr_hi, 1)
                for i in range(2):
                    gained(l, JB["ckv"] + i, xb, LAT_KV + 2 * i, G_KV + 2 * i, lat_hi)
                steps(l, 20, 26)

                def pooled(i):
                    b = BL["pool"] + i
                    block_ready(act, l, b)
                    for t in range(TT):
                        copy(up_[0][:, t, :], acc[b % 2][:, t, :], ACT.Copy,
                             scale=rstd["mix"][:, t:t + 1]).then_inc(upool_hi, 1)

                def diffs(i):
                    for k in range(2):
                        job = JB["diff"] + 2 * i + k
                        act.wait_ge(t_ready, JOBS * l + job + 1)
                        kt = DIFF + 4 * i + 2 * k
                        copy(xb[0][:, kt:kt + 2, :].rearrange("p a b -> p (a b)"), tps[:, job % T_BANKS, :],
                             ACT.Copy).then_inc(diff_hi, 1)

                pooled(0)
                steps(l, 26, 28)
                diffs(0)
                steps(l, 28, 34)
                pooled(1)
                steps(l, 34, 38)

                def qk(b, kt, number=None):
                    if number is None:
                        block_ready(act, l, b)
                    else:
                        act.wait_ge(pair_ready, 5 * l + number)
                    for k in range(2):
                        whole(l, b, k, xa[0][:, kt + 2 * k:kt + 2 * k + 2, :].rearrange("p a b -> p (a b)"), qk_hi)

                qk(BL["qnope"], Q_T, 1)
                qk(BL["qnope"] + 1, Q_T + 4)
                steps(l, 38, 40)
                diffs(1)
                steps(l, 40, 42)
                qk(BL["knope"], K_T, 2)
                qk(BL["knope"] + 1, K_T + 4)
                steps(l, 42, 44)
                for i in range(2):
                    job = JB["qrope"] + i
                    act.wait_ge(t_ready, JOBS * l + job + 1)
                    copy(qrt[0][:, 2 * i:2 * i + 2, :].rearrange("p a b -> p (a b)"), tps[:, job % T_BANKS, :],
                         ACT.Copy).then_inc(qr_hi, 1)
                steps(l, 44, 46)
                for i in range(2):
                    b = BL["v"] + i
                    if i == 0:
                        act.wait_ge(pair_ready, 5 * l + 3)
                    else:
                        block_ready(act, l, b)
                    for t in range(TT):
                        whole(l, b, t, v[0][:, t, i * BLK:(i + 1) * BLK], v_hi)
                steps(l, 46, 48)

                def pool_rows(n):
                    b = BL["poolw"] + n
                    block_ready(act, l, b)
                    for k in range(4):
                        kt = 4 * n + k
                        copy(xb[0][:, kt, :], acc[b % 2][:, k // 2, (k % 2) * S:(k % 2 + 1) * S], ACT.Copy,
                             scale=scalar_of(POOL_S + kt)).then_inc(ypool_hi, 1)

                for i in range(HEADS + 2):
                    if i == 0:
                        pool_rows(0)
                    if i == HEADS + 1:
                        steps(l, 49 + i, 50 + i)
                    if i >= 2:
                        act.wait_ge(t_ready, JOBS * l + JY[i - 2] + 1)
                        copy(xb[0][:, PKT + i - 2, :], tps[:, JY[i - 2] % T_BANKS, 0:S], ACT.Copy).then_inc(y_hi, 1)
                    if 1 <= i <= HEADS:
                        act.wait_ge(t_ready, JOBS * l + JT[i - 1] + 1)
                        copy(pt[0][:, :], tps[:, JT[i - 1] % T_BANKS, 0:3 * P], ACT.Copy).then_inc(pt_hi, 1)
                    if i < HEADS:
                        act.wait_ge(s_ready, HEADS * l + i + 1)
                        copy(prob[:, i % 2, 0:P], prob[:, i % 2, 0:P], ACT.Exp, bias=nmx[:, i % 2, 0:1],
                             scale=SCALE, accum_out=psums[:, i % 2, 0:1])
                        copy(prob[:, i % 2, P:3 * P], prob[:, i % 2, P:3 * P], ACT.Exp, bias=nmx[:, i % 2, 1:2],
                             scale=SCALE, accum_out=psums[:, i % 2, 1:2]).then_inc(e_done, 1)
                    if i == 0:
                        steps(l, 48, 50)
                    elif i == 1:
                        pool_rows(1)
                        steps(l, 50, 51)
                    elif i <= HEADS:
                        steps(l, 49 + i, 50 + i)

                def norm_job(job0, i, dst, gain):
                    gained(l, job0 + i, dst, 2 * i, gain + 2 * i, hT_hi)

                def out_job(j):
                    for i in (2 * j, 2 * j + 1):
                        norm_job(JB["ffn_norm"], i, xa, G_FFN)

                steps(l, 59, 66)
                squares(l, 0, 1)
                out_job(0)
                steps(l, 66, 70)
                squares(l, 1, 2)
                out_job(1)
                steps(l, 70, 78)
                squares(l, 2, 3)
                out_job(2)
                steps(l, 78, 86)
                squares(l, 3, 4)
                out_job(3)

                def split_u(l, v, m):
                    c = m // 2
                    act.wait_ge(raw_landed[c % RAW_SLOTS],
                                l * (CHUNKS // RAW_SLOTS * 16) + v * (UNIT_CHUNKS // RAW_SLOTS * 16)
                                + (c // RAW_SLOTS * 16 + 16))
                    act.wait_ge(w_used, l * (2 * CHUNKS) + v * UNIT_HALVES + (m + 1))
                    copy(w_hi[:, half_of(m), :], raw[:, c % RAW_SLOTS, (m % 2) * HALF:(m % 2 + 1) * HALF],
                         ACT.Copy).then_inc(hi_done, 1)

                def unit(l, u, v, with_down):
                    m0 = 2 * CH["ffn"] + (16 if with_down else 0)
                    b0 = BL["ffn"] + (2 if with_down else 0)

                    def go(a, b):
                        for m in range(a, b):
                            split_u(l, v, m0 + m + AHEAD)

                    def at_block(k):
                        block_ready(act, l, b0 + k, v)

                    def rows_out(k, dst):
                        at_block(k)
                        for t in range(TT):
                            copy(dst[:, t, :], acc[(b0 + k) % 2][:, t, :], ACT.Copy,
                                 scale=rstd["ffn"][:, t:t + 1]).then_inc(acc_free[(b0 + k) % 2], 1)

                    if with_down:
                        go(0, 2)
                        at_block(-1)
                        act.wait_ge(g_done, UNITS * l + u)
                        copy(gt[0][:, :, :], conv[:, :, :], ACT.Copy).then_inc(g_hi, 1)
                    go(2, 8)
                    if not with_down:
                        act.wait_ge(rstd_done, 5 * l + 5)
                    rows_out(0, gate_tok)
                    go(8, 13)
                    act.wait_ge(conv_done, UNITS * l + u + 1)
                    copy(sig[:, :, :], conv[:, :, :], ACT.Tanh, scale=0.5).then_inc(tanh_done, 1)
                    go(13, 16)
                    rows_out(1, up_tok)
                    if with_down:
                        go(16, 24)

                unit(l, 0, 0, False)
                with act.Fori(1, UNITS) as u:
                    unit(l, u, u - 1, True)
                act.wait_ge(g_done, UNITS * l + UNITS)
                copy(xa[0][:, 0:4, :], conv[:, :, :], ACT.Copy).then_inc(g_hi, 1)

                d0 = 2 * (CHUNKS - plan["n_blk"] * 4 - 2 - N_BLK)

                def ple_job(j):
                    for i in (2 * j, 2 * j + 1):
                        norm_job(JB["ple_norm"], i, xb, G_PLE)

                steps(l, d0, d0 + 1)
                act.wait_ge(t_ready, JOBS * l + JB["p"] + 1)
                copy(ppt[0][:, :, :].rearrange("p a b -> p (a b)"), tps[:, JB["p"] % T_BANKS, :], ACT.Copy).then_inc(
                    p_hi, 1)
                steps(l, d0 + 1, d0 + 3)
                e0 = d0 + 2 * N_BLK

                def pw_out(i):
                    for k in range(2):
                        b = BL["ple"] + 4 * i + k
                        if k == 0:
                            act.wait_ge(pair_ready, 5 * l + 4 + i)
                        else:
                            block_ready(act, l, b)
                        for t in range(TT):
                            copy(pw[:, i, t, k * BLK:(k + 1) * BLK], acc[b % 2][:, t, :], ACT.Copy).then_inc(
                                acc_free[b % 2], 1)

                def gate_tanh(j):
                    b = BL["ple"] + 2 + j + 2 * (j // 2)
                    block_ready(act, l, b)
                    if j == 0:
                        act.wait_ge(rstd_done, 5 * l + 6)
                    if j >= 2:
                        act.wait_ge(h_ready, 3 * N_BLK * l + N_BLK + 2 * N_BLK + j - 1)
                    for t in range(TT):
                        copy(sg[:, j % 2, t, :], acc[b % 2][:, t, :], ACT.Tanh,
                             scale=rstd["ple"][:, t:t + 1]).then_inc(acc_free[b % 2], 1)

                for j in range(N_BLK - 1):
                    squares(l, j, N_BLK + j + 1)
                    ple_job(j)
                    steps(l, d0 + 3 + 2 * j, d0 + 5 + 2 * j)
                squares(l, 3, 2 * N_BLK)
                steps(l, d0 + 9, e0 + 2)
                pw_out(0)
                ple_job(3)
                steps(l, e0 + 2, e0 + 12)
                gate_tanh(0)
                steps(l, e0 + 12, e0 + 14)
                squares(l, 0, 2 * N_BLK + 1)
                steps(l, e0 + 14, e0 + 20)
                gate_tanh(1)
                pw_out(1)
                squares(l, 1, 2 * N_BLK + 2)
                steps(l, e0 + 20, e0 + 30)
                gate_tanh(2)
                steps(l, e0 + 30, e0 + 32)
                squares(l, 2, 2 * N_BLK + 3)
                act.wait_ge(prm_ready, l + 3)
                for i in range(4):
                    mix_job(l + 1, i)
                steps(l, e0 + 32, e0 + 34)
                gate_tanh(3)
            squares(L, N_BLK - 1, 0)

        @block.vector
        def _(dve):
            n = [0]

            def step(ins):
                n[0] += 1
                ins.then_inc(dve_setup, 1)

            def after():
                dve.wait_ge(dve_setup, n[0])

            dve.sem_inc(h_ready, N_BLK)
            dve.sem_inc(lo_done, 2 * RAW_SLOTS)
            dve.sem_inc(acc_free[0], 2)
            dve.sem_inc(t_done, T_BANKS)
            dve.wait_ge(pool_setup, 8)
            step(dve.reciprocal(inv_cnt[:, :], inv_cnt[:, :]))
            for i in range(2):
                step(dve.memset(krt[i][ROPE:P, 0, :].bitcast(F32), 0.0))
                step(dve.memset(krt[i][0:ROPE, 1, :].bitcast(F32), 0.0))
            dve.wait_ge(pos_landed, 16)
            step(dve.tensor_copy(pos_f[:, :], pos_i[:, :]))
            after()
            dve.wait_ge(pool_setup, 10 + ROPE // 2)
            for t in range(TT):
                step(dve.tensor_scalar(ang[:, t, :], inv_freq[:, :], pos_f[:, t:t + 1], None, ALU.mult))
            after()
            for i in range(2):
                step(dve.tensor_scalar(turns[:, i], ang[:, :, :], float(1.0 / (2.0 * np.pi)), 0.25 * i, ALU.mult,
                                       ALU.add))
            after()
            magic = 1.5 * 2.0 ** 23
            step(dve.tensor_scalar(turns[:, :], turns[:, :], magic, None, ALU.add))
            after()
            step(dve.tensor_scalar(turns[:, :], turns[:, :], magic, None, ALU.subtract))
            after()
            parts = [6.28125]
            parts.append(float(np.float32(np.float64(2 * np.pi - parts[0]) // 2.0 ** -20 * 2.0 ** -20)))
            parts.append(float(np.float32(2 * np.pi - parts[0] - parts[1])))
            for i in range(2):
                step(dve.scalar_tensor_tensor(red[:, i], turns[:, i], -parts[0], ang[:, :, :], ALU.mult, ALU.add))
            after()
            for c in parts[1:]:
                step(dve.scalar_tensor_tensor(red[:, :], turns[:, :], -c, red[:, :], ALU.mult, ALU.add))
                after()
            step(dve.tensor_scalar(red[:, 1], red[:, 1], float(np.pi / 2), None, ALU.add))
            after()
            step(dve.tensor_scalar(red[:, :], red[:, :], 3.1415925, -3.1415925, ALU.min, ALU.max))
            assert n[0] == DVE_REDUCED
            dve.wait_ge(prm_t, 1)
            dve.tensor_copy(prm[:, 0:ROWS_G], acc[1][:, 0, 0:ROWS_G]).then_inc(prm_ready, 1)
            dve.wait_ge(prm_ready, 1)

            def split(l, m, v=None):
                c = m // 2
                if v is None:
                    base = l * (2 * CHUNKS)
                else:
                    base = l * (2 * CHUNKS) + v * UNIT_HALVES
                dve.wait_ge(hi_done, base + (m + 1))
                dve.wait_ge(w_used, base + (m + 1))
                dve.tensor_tensor(w_lo[:, half_of(m), :], raw[:, c % RAW_SLOTS, (m % 2) * HALF:(m % 2 + 1) * HALF],
                                  w_hi[:, half_of(m), :].bitcast(F32), ALU.subtract).then_inc(lo_done, 1)

            def steps(l, a, b):
                for m in range(a, b):
                    split(l, m + AHEAD)

            def lo(dst, src, hi, gain=None):
                if gain is None:
                    return dve.tensor_tensor(dst, src, hi.bitcast(F32), ALU.subtract)
                return dve.scalar_tensor_tensor(dst, src, gain, hi.bitcast(F32), ALU.mult, ALU.subtract)

            def gained(l, job, dst, kt, gain, hi_sem, value):
                dve.wait_ge(hi_sem, value)
                for i in range(2):
                    ins = lo(dst[1][:, kt + i, :], tps[:, job % T_BANKS, i * S:(i + 1) * S], dst[0][:, kt + i, :],
                             scalar_of(gain + i))
                ins.then_inc(t_done, 1)

            def mix_job(l, i):
                gained(l, JB["mix"] + i, xa, 2 * i, G_MIX + 2 * i, hT_hi, 3 * HJ * l + i + 1)

            mix_job(0, 0)
            mix_job(0, 1)
            split(0, 0)
            split(0, 1)
            mix_job(0, 2)
            mix_job(0, 3)
            dve.wait_ge(prm_t, 2)
            for l in range(L):
                step(dve.tensor_copy(prm_all[:, l, 0:G_Q], acc[1][:, l, 0:G_Q]))
            after()
            dve.sem_inc(acc_free[1], 2)
            dve.wait_ge(lat_landed, 16 * 2)
            dve.wait_ge(hT_hi, 4)
            dve.tensor_copy(prm, prm_all[:, 0, :]).then_inc(prm_ready, 1)

            dve.wait_ge(act_setup, 2)

            with dve.Fori(0, L) as l:
                dve.wait_ge(prm_ready, l + 2)
                steps(l, -2, 2)
                for i in range(4, 6):
                    mix_job(l, i)
                steps(l, 2, 4)
                for i in range(6, 8):
                    mix_job(l, i)
                steps(l, 4, 10)

                def latent(i):
                    dve.wait_ge(rstd_done, 5 * l + 3 + i)
                    for t in range(TT):
                        ins = dve.tensor_scalar(lat[:, i, t, :], lat[:, i, t, :],
                                                rstd[("q", "kv")[i]][:, t:t + 1], None, ALU.mult)
                    ins.then_inc(lat_norm, 1)

                latent(0)
                steps(l, 10, 12)
                for i in range(2):
                    gained(l, JB["cq"] + i, xb, LAT_Q + 2 * i, G_Q + 2 * i, lat_hi, 4 * l + i + 1)
                steps(l, 12, 18)
                latent(1)

                dve.wait_ge(acc_free[BL["kr"] % 2], BLOCKS * l + 2 * (BL["kr"] // 2 + 2))
                half = ROPE // 2
                x1, x2 = kr_in[:, :, 0:half], kr_in[:, :, half:ROPE]
                o1, o2 = kr_tok[:, :, 0:half], kr_tok[:, :, half:ROPE]
                dve.tensor_tensor(o1, x1, cos[:, :, :], ALU.mult)
                dve.tensor_tensor(kr_tmp[:, 0], x2, sin[:, :, :], ALU.mult)
                dve.tensor_tensor(o2, x2, cos[:, :, :], ALU.mult)
                dve.tensor_tensor(kr_tmp[:, 1], x1, sin[:, :, :], ALU.mult).then_inc(kr_step, 1)
                dve.wait_ge(kr_step, 3 * l + 1)
                dve.tensor_tensor(o1, o1, kr_tmp[:, 0], ALU.subtract)
                dve.tensor_tensor(o2, o2, kr_tmp[:, 1], ALU.add).then_inc(kr_step, 1)
                dve.wait_ge(kr_step, 3 * l + 2)
                dve.tensor_copy(kr_tok[:, :, ROPE:P], kr_tok[:, :, 0:ROPE]).then_inc(kr_step, 1)
                steps(l, 18, 20)
                dve.wait_ge(kr_hi, l + 1)
                bank = tps[:, JB["kr"] % T_BANKS, 0:S]
                lo(krt[1][0:ROPE, 0, :], bank[0:ROPE], krt[0][0:ROPE, 0, :])
                lo(krt[1][ROPE:P, 1, :], bank[ROPE:P], krt[0][ROPE:P, 1, :]).then_inc(t_done, 1)
                for i in range(2):
                    gained(l, JB["ckv"] + i, xb, LAT_KV + 2 * i, G_KV + 2 * i, lat_hi, 4 * l + 3 + i)
                steps(l, 20, 26)

                def pooled(i):
                    b = BL["pool"] + i
                    for t in range(TT):
                        dve.wait_ge(upool_hi, 2 * TT * l + TT * i + t + 1)
                        lo(up_[1][:, t, :], acc[b % 2][:, t, :], up_[0][:, t, :],
                           rstd["mix"][:, t:t + 1]).then_inc(acc_free[b % 2], 1)

                def diffs(i):
                    for k in range(2):
                        job = JB["diff"] + 2 * i + k
                        dve.wait_ge(diff_hi, 4 * l + 2 * i + k + 1)
                        kt = DIFF + 4 * i + 2 * k
                        two = lambda x: x[:, kt:kt + 2, :].rearrange("p a b -> p (a b)")
                        lo(two(xb[1]), tps[:, job % T_BANKS, :], two(xb[0])).then_inc(t_done, 1)

                pooled(0)
                steps(l, 26, 28)
                diffs(0)
                steps(l, 28, 34)
                pooled(1)
                steps(l, 34, 36)

                b = BL["qrope"]
                block_ready(dve, l, b)
                for t in range(TT):
                    q = acc[b % 2][:, t, :].rearrange("p (h c) -> p h c", c=ROPE)
                    o = qr_tok[:, t, :].rearrange("p (h c) -> p h c", c=ROPE)
                    tmp = [qr_tmp[:, i, :].rearrange("p (h c) -> p h c", c=half) for i in range(2)]
                    ct, st = (z[:, t, :].unsqueeze(1).broadcast_to([P, HEADS, half]) for z in (cos, sin))
                    q1, q2 = q[:, :, 0:half], q[:, :, half:ROPE]
                    o1, o2 = o[:, :, 0:half], o[:, :, half:ROPE]
                    dve.tensor_tensor(o1, q1, ct, ALU.mult)
                    dve.tensor_tensor(tmp[0], q2, st, ALU.mult).then_inc(qr_step, 1)
                    dve.tensor_tensor(o2, q2, ct, ALU.mult)
                    dve.tensor_tensor(tmp[1], q1, st, ALU.mult).then_inc(acc_free[b % 2], 1)
                    dve.wait_ge(qr_step, 3 * TT * l + 3 * t + 1)
                    dve.tensor_tensor(o1, o1, tmp[0], ALU.subtract).then_inc(qr_step, 1)
                    dve.wait_ge(acc_free[b % 2], BLOCKS * l + 2 * (b // 2 + 1) + t + 1)
                    dve.tensor_tensor(o2, o2, tmp[1], ALU.add).then_inc(qr_step, 1)
                    dve.wait_ge(qr_step, 3 * TT * l + 3 * t + 3)
                steps(l, 36, 38)

                def qk(b, kt, number):
                    for k in range(2):
                        dve.wait_ge(qk_hi, 8 * l + number + k + 1)
                        two = lambda x: x[:, kt + 2 * k:kt + 2 * k + 2, :].rearrange("p a b -> p (a b)")
                        lo(two(xa[1]), acc[b % 2][:, k, :], two(xa[0])).then_inc(acc_free[b % 2], 1)

                qk(BL["qnope"], Q_T, 0)
                qk(BL["qnope"] + 1, Q_T + 4, 2)
                steps(l, 38, 40)
                diffs(1)
                steps(l, 40, 42)
                qk(BL["knope"], K_T, 4)
                qk(BL["knope"] + 1, K_T + 4, 6)
                steps(l, 42, 44)
                for i in range(2):
                    job = JB["qrope"] + i
                    dve.wait_ge(qr_hi, 2 * l + i + 1)
                    two = lambda x: x[:, 2 * i:2 * i + 2, :].rearrange("p a b -> p (a b)")
                    lo(two(qrt[1]), tps[:, job % T_BANKS, :], two(qrt[0])).then_inc(t_done, 1)
                steps(l, 44, 46)
                for i in range(2):
                    b = BL["v"] + i
                    for t in range(TT):
                        dve.wait_ge(v_hi, 4 * l + 2 * i + t + 1)
                        lo(v[1][:, t, i * BLK:(i + 1) * BLK], acc[b % 2][:, t, :],
                           v[0][:, t, i * BLK:(i + 1) * BLK]).then_inc(acc_free[b % 2], 1)
                steps(l, 46, 48)

                def pool_rows(n):
                    b = BL["poolw"] + n
                    for i in range(4):
                        kt = 4 * n + i
                        if i % 2 == 0:
                            dve.wait_ge(ypool_hi, PKT * l + kt + 2)
                        ins = lo(xb[1][:, kt, :], acc[b % 2][:, i // 2, (i % 2) * S:(i % 2 + 1) * S],
                                 xb[0][:, kt, :], scalar_of(POOL_S + kt))
                        if i % 2:
                            ins.then_inc(acc_free[b % 2], 1)

                for i in range(HEADS + 2):
                    k = i % 2
                    if i < HEADS:
                        bank = tps[:, JS[i] % T_BANKS]
                        dve.wait_ge(t_ready, JOBS * l + JS[i] + 1)
                        dve.sem_inc(scores_seen, 1)
                        dve.tensor_tensor_reduce(prob[:, k, 0:P], bank[:, 0:P], mask[:, P:2 * P], 1.0, MASKED,
                                                 ALU.add, ALU.max, mx[:, k, 0:1])
                        dve.tensor_tensor_reduce(prob[:, k, P:3 * P], bank[:, P:3 * P], mask[:, :], 1.0, MASKED,
                                                 ALU.add, ALU.max, mx[:, k, 1:2]).then_inc(t_done, 1)
                        dve.wait_ge(t_done, JOBS * l + JS[i] + 1 + T_BANKS)
                        dve.tensor_scalar(nmx[:, k, :], mx[:, k, :], -SCALE, None, ALU.mult).then_inc(s_ready, 1)
                    if i == 0:
                        pool_rows(0)
                    if i == HEADS + 1:
                        steps(l, 49 + i, 50 + i)
                    if i >= 2:
                        dve.wait_ge(y_hi, HEADS * l + i - 1)
                        lo(xb[1][:, PKT + i - 2, :], tps[:, JY[i - 2] % T_BANKS, 0:S],
                           xb[0][:, PKT + i - 2, :]).then_inc(t_done, 1)
                    if 1 <= i <= HEADS:
                        dve.wait_ge(pt_hi, HEADS * l + i)
                        lo(pt[1][:, :], tps[:, JT[i - 1] % T_BANKS, 0:3 * P], pt[0][:, :]).then_inc(t_done, 1)
                    if i < HEADS:
                        dve.wait_ge(e_done, HEADS * l + i + 1)
                        dve.reciprocal(prec[:, k, :], psums[:, k, :]).then_inc(p_rec, 1)
                        dve.wait_ge(p_rec, HEADS * l + i + 1)
                        dve.tensor_scalar(prob[:, k, 0:P], prob[:, k, 0:P], prec[:, k, 0:1], None, ALU.mult)
                        dve.tensor_scalar(prob[:, k, P:3 * P], prob[:, k, P:3 * P], prec[:, k, 1:2], None,
                                          ALU.mult).then_inc(p_norm, 1)
                    if i == 0:
                        steps(l, 48, 50)
                    elif i == 1:
                        pool_rows(1)
                        steps(l, 50, 51)
                    elif i <= HEADS:
                        steps(l, 49 + i, 50 + i)

                def add_block(l, b, j, v, finished):
                    block_ready(dve, l, b, v)
                    for t in range(TT):
                        hb = h[:, t, j * BLK:(j + 1) * BLK]
                        dve.tensor_tensor(hb, acc[b % 2][:, t, :], hb, ALU.add).then_inc(acc_free[b % 2], 1)
                    if finished:
                        dve.wait_ge(acc_free[b % 2], BLOCKS * l + 2 * (b // 2 + 2))
                        dve.sem_inc(h_ready, 1)

                def out_job(j):
                    for i in (2 * j, 2 * j + 1):
                        gained(l, JB["ffn_norm"] + i, xa, 2 * i, G_FFN + 2 * i, hT_hi, 3 * HJ * l + HJ + i + 1)

                steps(l, 59, 64)
                add_block(l, BL["out"], 0, None, True)
                steps(l, 64, 66)
                out_job(0)
                steps(l, 66, 68)
                add_block(l, BL["out"] + 1, 1, None, True)
                steps(l, 68, 70)
                out_job(1)
                steps(l, 70, 76)
                add_block(l, BL["out"] + 2, 2, None, True)
                steps(l, 76, 78)
                out_job(2)
                steps(l, 78, 84)
                add_block(l, BL["out"] + 3, 3, None, True)
                steps(l, 84, 86)
                out_job(3)

                def unit(l, u, vv, with_down):
                    m0 = 2 * CH["ffn"] + (16 if with_down else 0)
                    b0 = BL["ffn"] + (2 if with_down else 0)
                    j0 = JB["ffn"] + (4 if with_down else 0)
                    c0 = 8 * UNITS * l + 8 * u

                    def go(a, b):
                        for m in range(a, b):
                            split(l, m0 + m + AHEAD, vv)

                    def job_ready(k):
                        dve.wait_ge(t_ready, JOBS * l + 4 * vv + (j0 + k + 1))

                    def tap(t, ft):
                        return prm[:, bass.ds(4 * u + (TAP[t] + ft), 1)]

                    def gate_t(ft):
                        return tps[:, (j0 + ft // 2) % T_BANKS, (ft % 2) * S:(ft % 2 + 1) * S]

                    if with_down:
                        go(0, 2)
                        dve.wait_ge(g_hi, UNITS * l + u)
                        lo(gt[1][:, :, :], conv[:, :, :], gt[0][:, :, :]).then_inc(g_lo, 1)
                    go(2, 11)
                    for ft in range(4):
                        if ft % 2 == 0:
                            job_ready(ft // 2)
                        dve.tensor_scalar(conv[:, ft, :], gate_t(ft), tap(2, ft),
                                          prm[:, bass.ds(4 * u + (BIAS + ft), 1)], ALU.mult,
                                          ALU.add).then_inc(conv_step, 1)
                    for ft in range(4):
                        dve.wait_ge(conv_step, c0 + (ft + 1))
                        dve.scalar_tensor_tensor(conv[:, ft, 1:S], gate_t(ft)[:, 0:S - 1], tap(1, ft), conv[:, ft, 1:S],
                                                 ALU.mult, ALU.add).then_inc(conv_step, 1)
                    for ft in range(4):
                        dve.wait_ge(conv_step, c0 + (4 + ft + 1))
                        ins = dve.scalar_tensor_tensor(conv[:, ft, 2:S], gate_t(ft)[:, 0:S - 2], tap(0, ft),
                                                       conv[:, ft, 2:S], ALU.mult, ALU.add)
                        if ft % 2:
                            ins.then_inc(t_done, 1)
                    dve.wait_ge(t_done, JOBS * l + 4 * vv + (j0 + 2 + T_BANKS))
                    dve.sem_inc(conv_done, 1)
                    go(11, 14)
                    dve.wait_ge(tanh_done, UNITS * l + u + 1)
                    dve.scalar_tensor_tensor(conv[:, :, :], sig[:, :, :], 1.0, conv[:, :, :], ALU.add,
                                             ALU.mult).then_inc(silu_done, 1)
                    go(14, 16)

                    def gated():
                        dve.wait_ge(silu_done, UNITS * l + u + 1)
                        for k in range(2):
                            job_ready(2 + k)
                            two = conv[:, 2 * k:2 * k + 2, :].rearrange("p a b -> p (a b)")
                            dve.scalar_tensor_tensor(two, tps[:, (j0 + 2 + k) % T_BANKS, :], 0.5, two, ALU.mult,
                                                     ALU.mult).then_inc(t_done, 1)
                        dve.wait_ge(t_done, JOBS * l + 4 * vv + (j0 + 4 + T_BANKS))
                        dve.sem_inc(g_done, 1)

                    if with_down:
                        go(16, 19)
                        add_block(l, b0 + 2, 0, vv, False)
                        gated()
                        go(19, 21)
                        add_block(l, b0 + 3, 1, vv, False)
                        go(21, 23)
                        add_block(l, b0 + 4, 2, vv, False)
                        go(23, 24)
                        add_block(l, b0 + 5, 3, vv, False)
                    else:
                        gated()

                unit(l, 0, 0, False)
                with dve.Fori(1, UNITS) as u:
                    unit(l, u, u - 1, True)

                d0 = 2 * (CHUNKS - 4 * N_BLK - 2 - N_BLK)
                e0 = d0 + 2 * N_BLK
                bd = BL["ple"] - N_BLK

                def ple_job(j):
                    for i in (2 * j, 2 * j + 1):
                        gained(l, JB["ple_norm"] + i, xb, 2 * i, G_PLE + 2 * i, hT_hi, 3 * HJ * l + 2 * HJ + i + 1)

                steps(l, d0, d0 + 1)
                dve.wait_ge(p_hi, l + 1)
                two = lambda x: x[:, :, :].rearrange("p a b -> p (a b)")
                lo(two(ppt[1]), tps[:, JB["p"] % T_BANKS, :], two(ppt[0])).then_inc(t_done, 1)
                steps(l, d0 + 1, d0 + 2)
                for j in range(N_BLK):
                    add_block(l, bd + j, j, None, True)
                    steps(l, d0 + 2 + 2 * j, d0 + 3 + 2 * j)
                    ple_job(j)
                    steps(l, d0 + 3 + 2 * j, d0 + 4 + 2 * j)

                def gate(j):
                    b = BL["ple"] + 2 + j + 2 * (j // 2)
                    dve.wait_ge(acc_free[b % 2], BLOCKS * l + 2 * (b // 2 + 2))
                    if j % 2 == 0:
                        bp = BL["ple"] + 4 * (j // 2) + 1
                        dve.wait_ge(acc_free[bp % 2], BLOCKS * l + 2 * (bp // 2 + 2))
                    pj = slice((j % 2) * BLK, (j % 2 + 1) * BLK)
                    for t in range(TT):
                        sgt = sg[:, j % 2, t, :]
                        dve.scalar_tensor_tensor(sgt, sgt, 1.0, pw[:, j // 2, t, pj], ALU.add,
                                                 ALU.mult).then_inc(ple_step, 1)
                    for t in range(TT):
                        hb = h[:, t, j * BLK:(j + 1) * BLK]
                        dve.wait_ge(ple_step, TT * N_BLK * l + TT * j + t + 1)
                        ins = dve.scalar_tensor_tensor(hb, sg[:, j % 2, t, :], 0.5, hb, ALU.mult, ALU.add)
                    ins.then_inc(h_ready, 1)

                steps(l, e0 + 2, e0 + 12)
                gate(0)
                steps(l, e0 + 12, e0 + 20)
                gate(1)
                steps(l, e0 + 20, e0 + 30)
                gate(2)
                steps(l, e0 + 30, e0 + 32)
                dve.tensor_copy(prm, prm_all[:, bass.ds(l + 1, 1), :].rearrange("p a b -> p (a b)")).then_inc(
                    prm_ready, 1)
                dve.wait_ge(prm_ready, l + 3)
                for i in range(4):
                    mix_job(l + 1, i)
                steps(l, e0 + 32, e0 + 34)
                gate(3)

            dve.wait_ge(fin_landed, 16)
            dve.wait_ge(rstd_done, 5 * L + 2)
            dve.wait_ge(h_ready, 3 * N_BLK * L + N_BLK)
            for j in range(N_BLK):
                for t in range(TT):
                    hb = h[:, t, j * BLK:(j + 1) * BLK]
                    dve.scalar_tensor_tensor(hb, hb, rstd["final"][:, t:t + 1], fin_g[:, j * BLK:(j + 1) * BLK],
                                             ALU.mult, ALU.mult).then_inc(fin_done, 1)

        @block.tensor
        def _(pe):
            pe.sem_inc(w_used, HALF_SLOTS)
            pe.wait_ge(rows_landed, 16 * 4)
            pe.wait_ge(pool_setup, 9)
            for l in range(L):
                ins = pe.transpose(acc[1][:, l, 0:ROWS_G], rows_g[:, l, :], ident[0:ROWS_G, 0:ROWS_G])
            ins.then_inc(prm_t, 1)

            def three(dst, a_hi, a_lo, b_hi, b_lo, first, last):
                pe.matmul(dst, a_hi, b_hi, start=first, stop=False)
                pe.matmul(dst, a_lo, b_hi, start=False, stop=False)
                return pe.matmul(dst, a_hi, b_lo, start=False, stop=last)

            def halves(l, m, v=None):
                base = l * (2 * CHUNKS) + (2 * RAW_SLOTS + m + 1) if v is None else \
                    l * (2 * CHUNKS) + v * UNIT_HALVES + (2 * RAW_SLOTS + m + 1)
                pe.wait_ge(lo_done, base)
                return w_hi[:, half_of(m), :], w_lo[:, half_of(m), :]

            def free_acc(l, b, v=None):
                if v is None:
                    pe.wait_ge(acc_free[b % 2], BLOCKS * l + 2 * (b // 2 + 1))
                else:
                    pe.wait_ge(acc_free[b % 2], BLOCKS * l + (2 + N_BLK) * v + 2 * (b // 2 + 1))

            def square_half(l, m, b, x, kt, first, last, v=None):
                hi, lo = halves(l, m, v)
                if first:
                    free_acc(l, b, v)
                for k in range(2):
                    cols = slice(k * BLK, (k + 1) * BLK)
                    for t in range(TT):
                        tok = slice(t * P, (t + 1) * P)
                        ins = three(acc[b % 2][:, t, :], x[0][:, kt + k, tok], x[1][:, kt + k, tok], hi[:, cols],
                                    lo[:, cols], first and k == 0, last and k == 1)
                ins.then_inc(w_used, 1)

            def square_halves(l, m, b, x, a, z, v=None):
                for i in range(a, z):
                    square_half(l, m + i, b, x, 2 * i, i == 0, i == KT // 2 - 1, v)

            def new_job(l, job, v=None):
                pe.wait_ge(t_done, JOBS * l + (job + 1) if v is None else JOBS * l + 4 * v + (job + 1))
                return tps[:, job % T_BANKS]

            def jobs_split(l, job):
                pe.wait_ge(t_done, JOBS * l + (job + 1 + T_BANKS))

            def block_split(l, b, v=None):
                if v is None:
                    pe.wait_ge(acc_free[b % 2], BLOCKS * l + 2 * (b // 2 + 2))
                else:
                    pe.wait_ge(acc_free[b % 2], BLOCKS * l + (2 + N_BLK) * v + 2 * (b // 2 + 2))

            def turn(l, job, tiles, v=None):
                bank = new_job(l, job, v)
                for t in range(TT):
                    for i in range(2):
                        ins = pe.transpose(bank[:, i * S + t * P:i * S + (t + 1) * P], tiles(t, i), ident[:, :])
                ins.then_inc(t_ready, 1)

            def turn_h(l, job0, i):
                turn(l, job0 + i, lambda t, k: h[:, t, (2 * i + k) * P:(2 * i + k + 1) * P])

            for i in range(4):
                if i % 2 == 0:
                    pe.wait_ge(x_landed[i // 2], 16)
                turn_h(0, JB["mix"], i)
            pe.wait_ge(conv_landed, 16 * 3)
            pe.wait_ge(prm_ready, 1)
            for l in range(L):
                pe.transpose(acc[1][:, l, TAP[0]:TAP[2]], rows_c[0][:, l, :], ident[0:2 * FKT, 0:2 * FKT])
                ins = pe.transpose(acc[1][:, l, TAP[2]:G_Q], rows_c[1][:, l, :], ident[0:2 * FKT, 0:2 * FKT])
            ins.then_inc(prm_t, 1)

            with pe.Fori(0, L) as l:
                m, b = 0, BL["cq"]
                for i in range(4):
                    jobs_split(l, JB["mix"] + 2 * i + 1)
                    square_halves(l, m, b, xa, 2 * i, 2 * i + 2)
                    if i < 2:
                        pe.wait_ge(x_landed[i + 2], 16)
                        pe.wait_ge(h_ready, 3 * N_BLK * l + i + 3)
                        turn_h(l, JB["mix"], 4 + 2 * i)
                        turn_h(l, JB["mix"], 5 + 2 * i)
                m, b = 8, BL["ckv"]
                square_halves(l, m, b, xa, 0, 4)

                def turn_lat(i, job):
                    pe.wait_ge(lat_norm, 2 * l + i + 1)
                    for k in range(2):
                        turn(l, job + k, lambda t, n: lat[:, i, t, :].rearrange("p (f k) -> p f k", k=LKT)[
                            :, :, 2 * k + n])

                turn_lat(0, JB["cq"])
                square_halves(l, m, b, xa, 4, 8)
                m, b = 2 * CH["kr"], BL["kr"]
                hi, lo = halves(l, m)
                free_acc(l, b)
                for t in range(TT):
                    tok = slice(t * P, (t + 1) * P)
                    for k in range(KT):
                        if (t, k) == (TT - 1, KT - 1):
                            halves(l, m + 1)
                        cols = slice(k * ROPE, (k + 1) * ROPE)
                        ins = three(acc[b % 2][:, t, 0:ROPE], xa[0][:, k, tok], xa[1][:, k, tok], hi[:, cols],
                                    lo[:, cols], k == 0, k == KT - 1)
                ins.then_inc(w_used, 2)
                m, b = 2 * CH["pool"], BL["pool"]
                square_halves(l, m, b, xa, 0, 2)
                pe.wait_ge(kr_step, 3 * l + 3)
                bank = new_job(l, JB["kr"])
                for t in range(TT):
                    ins = pe.transpose(bank[:, t * P:(t + 1) * P], kr_tok[:, t, :], ident[:, :])
                ins.then_inc(t_ready, 1)
                turn_lat(1, JB["ckv"])
                square_halves(l, m, b, xa, 2, 8)

                def diffs(i):
                    if i == 0:
                        pe.wait_ge(pool_setup, POOL_SETUP)
                    block_split(l, BL["pool"] + i)
                    for k in range(2):
                        g = 2 * i + k
                        job = JB["diff"] + g
                        bank = new_job(l, job)
                        for n in range(2):
                            f = slice((2 * k + n) * P, (2 * k + n + 1) * P)
                            d = bank[:, n * S:(n + 1) * S]
                            pe.matmul(d, up_[0][:, 0, f], band_hi[:, g, 0:S], start=True, stop=False)
                            pe.matmul(d, up_[1][:, 0, f], band_hi[:, g, 0:S], start=False, stop=False)
                            pe.matmul(d[:, 0:16], up_[0][:, 0, f], band_lo[:, g, :], start=False, stop=False)
                            pe.matmul(d[:, P:S], up_[0][:, 1, f], band_hi[:, g, S:S + P], start=False, stop=False)
                            ins = pe.matmul(d[:, P:S], up_[1][:, 1, f], band_hi[:, g, S:S + P], start=False,
                                            stop=True)
                        ins.then_inc(t_ready, 1)

                m, b = m + 8, b + 1
                square_halves(l, m, b, xa, 0, 2)
                diffs(0)
                square_halves(l, m, b, xa, 2, 8)
                m, b = 2 * CH["uq"], BL["qrope"]
                jobs_split(l, JB["cq"] + 1)
                free_acc(l, b)
                for i in range(2):
                    hi, lo = halves(l, m + i)
                    for k in range(2):
                        cols = slice(k * BLK, (k + 1) * BLK)
                        for t in range(TT):
                            tok = slice(t * P, (t + 1) * P)
                            kt = 2 * i + k
                            ins = three(acc[b % 2][:, t, :], xb[0][:, LAT_Q + kt, tok], xb[1][:, LAT_Q + kt, tok],
                                        hi[:, cols], lo[:, cols], kt == 0, kt == LKT - 1)
                    ins.then_inc(w_used, 1)

                def by_feature(m, b, lat_t):
                    parts = []
                    for n in range(2):
                        free_acc(l, b + n)
                        for i in range(2):
                            for k in range(LKT):
                                if n == 0 and i == 0:
                                    parts.append(halves(l, m + k))
                                hi, lo = parts[k]
                                for bank in range(2):
                                    dst = acc[(b + n) % 2][:, bank, i * S:(i + 1) * S]
                                    hd = 4 * n + 2 * bank + i
                                    cols = slice(hd * NOPE, (hd + 1) * NOPE)
                                    ins = three(dst, hi[:, cols], lo[:, cols], xb[0][:, lat_t + k, :],
                                                xb[1][:, lat_t + k, :], k == 0, k == LKT - 1)
                                if n == 1 and i == 1:
                                    ins.then_inc(w_used, 1)
                        if n == 0:
                            ins.then_inc(pair_ready, 1)

                m += 2
                by_feature(m, BL["qnope"], LAT_Q)
                diffs(1)
                jobs_split(l, JB["ckv"] + 1)
                m += LKT
                by_feature(m, BL["knope"], LAT_KV)
                pe.wait_ge(qr_step, 3 * TT * l + 3 * TT)
                for i in range(2):
                    turn(l, JB["qrope"] + i, lambda t, n: qr_tok[:, t, (2 * i + n) * P:(2 * i + n + 1) * P])
                m, b = m + LKT, BL["v"]
                parts = []
                for n in range(2):
                    free_acc(l, b + n)
                    for k in range(LKT):
                        if n == 0:
                            parts.append(halves(l, m + k))
                        hi, lo = parts[k]
                        cols = slice(n * BLK, (n + 1) * BLK)
                        for t in range(TT):
                            tok = slice(t * P, (t + 1) * P)
                            ins = three(acc[(b + n) % 2][:, t, :], xb[0][:, LAT_KV + k, tok],
                                        xb[1][:, LAT_KV + k, tok], hi[:, cols], lo[:, cols], k == 0, k == LKT - 1)
                        if n == 1:
                            ins.then_inc(w_used, 1)
                    if n == 0:
                        ins.then_inc(pair_ready, 1)

                def scores(i):
                    bank = new_job(l, JS[i]) if i > 0 else tps[:, JS[0] % T_BANKS]
                    for t in range(TT):
                        tok = slice(t * P, (t + 1) * P)
                        nk = (t + 1) * P
                        dst = bank[:, t * P:t * P + nk]
                        three(dst, xa[0][:, Q_T + i, tok], xa[1][:, Q_T + i, tok], xa[0][:, K_T + i, 0:nk],
                              xa[1][:, K_T + i, 0:nk], True, False)
                        ins = three(dst, qrt[0][:, i // 2, tok], qrt[1][:, i // 2, tok], krt[0][:, i % 2, 0:nk],
                                    krt[1][:, i % 2, 0:nk], False, True)
                    ins.then_inc(t_ready, 1)

                def outputs(i):
                    assert JT[i] >= JY[i] - T_BANKS
                    jobs_split(l, JT[i])
                    bank = tps[:, JY[i] % T_BANKS]
                    f = slice(i * VDIM, (i + 1) * VDIM)
                    three(bank[:, 0:S], v[0][:, 0, f], v[1][:, 0, f], pt[0][:, 0:S], pt[1][:, 0:S], True, False)
                    three(bank[:, P:S], v[0][:, 1, f], v[1][:, 1, f], pt[0][:, S:3 * P], pt[1][:, S:3 * P],
                          False, True).then_inc(t_ready, 1)

                def probs(i):
                    pe.wait_ge(p_norm, HEADS * l + i + 1)
                    bank = new_job(l, JT[i])
                    for n in range(3):
                        ins = pe.transpose(bank[:, n * P:(n + 1) * P], prob[:, i % 2, n * P:(n + 1) * P],
                                           ident[:, :])
                    ins.then_inc(t_ready, 1)

                def pool_out(i):
                    b = BL["poolw"] + i
                    hi, lo = halves(l, 2 * (CH["poolw"] + i))
                    free_acc(l, b)
                    for g in range(2):
                        for n in range(2):
                            dst = acc[b % 2][:, g, n * S:(n + 1) * S]
                            for k in range(2):
                                if g == n == k == 1:
                                    halves(l, 2 * (CH["poolw"] + i) + 1)
                                cols = slice((2 * g + k) * S + n * P, (2 * g + k) * S + (n + 1) * P)
                                d = DIFF + 4 * i + 2 * g + k
                                ins = three(dst, hi[:, cols], lo[:, cols], xb[0][:, d, :], xb[1][:, d, :], k == 0,
                                            k == 1)
                    ins.then_inc(w_used, 2)

                jobs_split(l, JB["qrope"] + 1)
                block_split(l, BL["v"])
                m_out, b_out = 2 * CH["out"], BL["out"]
                for i in range(HEADS + 2):
                    if i < HEADS:
                        scores(i)
                    if 2 <= i <= HEADS:
                        outputs(i - 2)
                    if 1 <= i <= HEADS:
                        probs(i - 1)
                    if i == 0:
                        pool_out(0)
                        pool_out(1)
                    elif i <= HEADS:
                        j, k = (i - 1) // 4, (i - 1) % 4
                        if j == 0 and k == 2:
                            block_split(l, BL["poolw"] + 1)
                        square_half(l, m_out + i - 1, b_out + j, xb, 2 * k, k == 0, False)
                m_out += HEADS
                for j in range(2):
                    for k in range(4):
                        if j == 0 and k in (0, 3):
                            jobs_split(l, JY[HEADS - 3 if k == 0 else HEADS - 1])
                        square_half(l, m_out, b_out + j, xb, 8 + 2 * k, False, k == 3)
                        m_out += 1
                        if j == 0 and k == 0:
                            outputs(HEADS - 1)
                        if j == 1 and k == 1:
                            pe.wait_ge(h_ready, 3 * N_BLK * l + N_BLK + 1)
                            turn_h(l, JB["ffn_norm"], 0)
                            turn_h(l, JB["ffn_norm"], 1)
                square_halves(l, m_out, b_out + 2, xb, 0, 2)
                pe.wait_ge(h_ready, 3 * N_BLK * l + N_BLK + 2)
                turn_h(l, JB["ffn_norm"], 2)
                turn_h(l, JB["ffn_norm"], 3)
                square_halves(l, m_out, b_out + 2, xb, 2, 8)
                m_out += 8
                square_halves(l, m_out, b_out + 3, xb, 0, 2)
                pe.wait_ge(h_ready, 3 * N_BLK * l + N_BLK + 3)
                turn_h(l, JB["ffn_norm"], 4)
                turn_h(l, JB["ffn_norm"], 5)
                square_halves(l, m_out, b_out + 3, xb, 2, 8)

                def down(m, b, g, v=None):
                    for i in range(2):
                        hi, lo = halves(l, m + i, v)
                        if i == 0:
                            free_acc(l, b, v)
                        for k in range(2):
                            cols = slice(k * BLK, (k + 1) * BLK)
                            for t in range(TT):
                                tok = slice(t * P, (t + 1) * P)
                                ft = 2 * i + k
                                ins = three(acc[b % 2][:, t, :], g[0][:, ft, tok], g[1][:, ft, tok], hi[:, cols],
                                            lo[:, cols], ft == 0, ft == 3)
                        ins.then_inc(w_used, 1)
                        yield i

                def unit(u, v, with_down):
                    m0 = 2 * CH["ffn"] + (16 if with_down else 0)
                    b0 = BL["ffn"] + (2 if with_down else 0)
                    j0 = JB["ffn"] + (4 if with_down else 0)

                    def turn_rows(rows, b, k):
                        block_split(l, b, v)
                        for i in range(2):
                            turn(l, j0 + k + i, lambda t, n: rows[:, t, (2 * i + n) * P:(2 * i + n + 1) * P], v)

                    if with_down:
                        square_halves(l, m0, b0, xa, 0, 8, v)
                    else:
                        square_halves(l, m0, b0, xa, 0, 2, v)
                        pe.wait_ge(h_ready, 3 * N_BLK * l + N_BLK + 4)
                        turn_h(l, JB["ffn_norm"], 6)
                        turn_h(l, JB["ffn_norm"], 7)
                        square_halves(l, m0, b0, xa, 2, 6, v)
                        jobs_split(l, JB["ffn_norm"] + 7)
                        square_halves(l, m0, b0, xa, 6, 8, v)
                    square_halves(l, m0 + 8, b0 + 1, xa, 0, 3, v)
                    turn_rows(gate_tok, b0, 0)
                    square_halves(l, m0 + 8, b0 + 1, xa, 3, 8, v)
                    if with_down:
                        pe.wait_ge(g_lo, UNITS * l + u)
                        for j in range(N_BLK):
                            for i in down(m0 + 16 + 2 * j, b0 + 2 + j, gt, v):
                                if j == 1 and i == 0:
                                    turn_rows(up_tok, b0 + 1, 2)
                    else:
                        turn_rows(up_tok, b0 + 1, 2)

                jobs_split(l, JB["ffn_norm"] + 5)
                unit(0, 0, False)
                with pe.Fori(1, UNITS) as u:
                    unit(u, u - 1, True)
                m, b = 2 * (CH["ple"] - N_BLK), BL["ple"] - N_BLK
                pe.wait_ge(g_lo, UNITS * l + UNITS)
                for j in range(N_BLK):
                    for i in down(m + 2 * j, b + j, xa):
                        if i == 0 and j == 0:
                            pe.wait_ge(p_landed, 16 * l + 16)
                            turn(l, JB["p"], lambda t, n: p_tok[:, t, n * P:(n + 1) * P])
                        elif i == 0:
                            pe.wait_ge(h_ready, 3 * N_BLK * l + N_BLK + N_BLK + j)
                            turn_h(l, JB["ple_norm"], 2 * j - 2)
                            turn_h(l, JB["ple_norm"], 2 * j - 1)

                m, b = 2 * CH["ple"], BL["ple"]
                jobs_split(l, JB["p"])
                for i in range(2):
                    parts = [halves(l, m), None]
                    for n in range(2):
                        free_acc(l, b + n)
                        cols = slice(n * BLK, (n + 1) * BLK)
                        for k in range(2):
                            if n == 0 and k == 1:
                                parts[1] = halves(l, m + 1)
                            hi, lo = parts[k]
                            for t in range(TT):
                                tok = slice(t * P, (t + 1) * P)
                                ins = three(acc[(b + n) % 2][:, t, :], ppt[0][:, k, tok], ppt[1][:, k, tok],
                                            hi[:, cols], lo[:, cols], k == 0, k == 1)
                            if n == 1:
                                ins.then_inc(w_used, 1)
                        if n == 0:
                            ins.then_inc(pair_ready, 1)
                    m, b = m + 2, b + 2
                    if i == 0:
                        pe.wait_ge(h_ready, 3 * N_BLK * l + N_BLK + 2 * N_BLK)
                        turn_h(l, JB["ple_norm"], 6)
                        turn_h(l, JB["ple_norm"], 7)
                        jobs_split(l, JB["ple_norm"] + 5)
                    for j in range(2):
                        square_halves(l, m, b, xb, 0, 6)
                        if i == 0 and j == 0:
                            jobs_split(l, JB["ple_norm"] + 7)
                        if i == 1 and j == 1:
                            pe.wait_ge(h_ready, 3 * N_BLK * (l + 1) + 2)
                            for k in range(4):
                                turn_h(l + 1, JB["mix"], k)
                        square_halves(l, m, b, xb, 6, 8)
                        m, b = m + 8, b + 1


_INS = ['x', 'p', 'positions', 'norm_mix_g', 'w_in', 'pool_w', 'pool_scale', 'q_norm_g', 'w_uq', 'kv_norm_g',
        'w_ukv', 'w_out', 'norm_ffn_g', 'w_up', 'conv_w', 'conv_b', 'w_down', 'norm_ple_g', 'w_ple',
        'w_ple_gate', 'final_norm_g']


def kernel(**inputs):
    import concourse.bacc as _bacc
    from concourse.bass_utils import run_bass_kernel_spmd as _run

    nc = _bacc.Bacc("TRN2", target_bir_lowering=False, num_devices=1)
    arrays, args = {}, []
    for name in _INS:
        a = np.ascontiguousarray(inputs[name])
        arrays[f"in_{name}"] = a
        args.append(nc.dram_tensor(f"in_{name}", a.shape, mybir.dt.from_np(a.dtype), kind="ExternalInput").ap())
    out = nc.dram_tensor("out_0", arrays["in_x"].shape, F32, kind="ExternalOutput").ap()
    build(nc, *args, out)
    r = _run(nc, [arrays], core_ids=[0])
    return r.results[0]["out_0"]
```
